# Optimizing a Trainium2 kernel written in Bass

```python
import math
import jax, jax.numpy as jnp
from jax import lax
import numpy as np

D_MODEL = 1024
BATCH = 1
SEQ = 256
DEPTH = 2

CHUNK = 128
A_GROUPS = 4
A_GROUP_DIM = 128
A_WIDTH = A_GROUPS * A_GROUP_DIM
B_HEADS = 4
B_HEAD_DIM = 128
B_WIDTH = B_HEADS * B_HEAD_DIM
B_ROT = B_HEAD_DIM // 4
IDX_HEADS = 4
IDX_DIM = 64
IDX_ROT = IDX_DIM // 4
TOPK_MAX = 256
Q_BLOCK = 128
C_WIDTH = 512
CONV_WIDTH = 3
N_BRANCH = 3
D_IN = 2 * A_WIDTH + 3 * B_WIDTH + IDX_HEADS * IDX_DIM + IDX_DIM + IDX_HEADS + 3 * C_WIDTH + N_BRANCH * D_MODEL
N_GROUPS = 4
EXP_PER_GROUP = 8
N_EXPERTS = N_GROUPS * EXP_PER_GROUP
TOP_K_EXP = 2
D_FF_EXPERT = 512
MOE_BLOCK = 128

ROPE_THETA = 500000.0
EPS = 1e-6
NEG = -1e30

kernel_name = "hybrid_gmlp_dsa_shortconv_hiermoe"

def rms_norm(x, g):
    xf = x.astype(jnp.float32)
    y = xf * lax.rsqrt(jnp.mean(xf * xf, axis=-1, keepdims=True) + EPS)
    return (y * g.astype(jnp.float32)).astype(x.dtype)

def layer_norm_noaffine(x):
    xf = x.astype(jnp.float32)
    mu = jnp.mean(xf, axis=-1, keepdims=True)
    var = jnp.mean(jnp.square(xf - mu), axis=-1, keepdims=True)
    return ((xf - mu) * lax.rsqrt(var + EPS)).astype(x.dtype)

def partial_rope(x, positions, rot_dim):
    half = rot_dim // 2
    inv_freq = jnp.float32(ROPE_THETA) ** (-jnp.arange(half, dtype=jnp.float32) * 2.0 / rot_dim)
    ang = positions.astype(jnp.float32)[..., None] * inv_freq
    cos = jnp.cos(ang)[:, :, None, :].astype(x.dtype)
    sin = jnp.sin(ang)[:, :, None, :].astype(x.dtype)
    x1 = x[..., :half]
    x2 = x[..., half:rot_dim]
    rest = x[..., rot_dim:]
    return jnp.concatenate([x1 * cos - x2 * sin, x1 * sin + x2 * cos, rest], axis=-1)

def gmlp_spatial(u, v, ws, bs):
    bsz, s, _ = u.shape
    n = s // CHUNK
    u = jax.nn.gelu(u)
    v = layer_norm_noaffine(jax.nn.gelu(v))
    vc = v.reshape(bsz, n, CHUNK, A_GROUPS, A_GROUP_DIM)
    causal = jnp.tril(jnp.ones((CHUNK, CHUNK), dtype=bool))
    wsm = jnp.where(causal[None], ws, jnp.zeros_like(ws))
    vm = jnp.einsum('gts,bnsgc->bntgc', wsm, vc) + bs.T[None, None, :, :, None]
    return u * vm.reshape(bsz, s, A_WIDTH)

def dsa_attention(q, k, v, qi, ki, wi, positions):
    bsz, s, _ = q.shape
    nblk = s // Q_BLOCK
    n_sel = min(TOPK_MAX, s // 4)
    q = partial_rope(q.reshape(bsz, s, B_HEADS, B_HEAD_DIM), positions, B_ROT)
    k = partial_rope(k.reshape(bsz, s, B_HEADS, B_HEAD_DIM), positions, B_ROT)
    v = v.reshape(bsz, s, B_HEADS, B_HEAD_DIM)
    qi = partial_rope(qi.reshape(bsz, s, IDX_HEADS, IDX_DIM), positions, IDX_ROT)
    ki = partial_rope(ki.reshape(bsz, s, 1, IDX_DIM), positions, IDX_ROT)[:, :, 0]
    wi = wi * (IDX_HEADS ** -0.5)
    key_pos = jnp.arange(s, dtype=jnp.int32)

    def to_blocks(a):
        return a.reshape(bsz, nblk, Q_BLOCK, *a.shape[2:]).swapaxes(0, 1)

    def block(args):
        qb, qib, wib, blk = args
        t = blk * Q_BLOCK + jnp.arange(Q_BLOCK, dtype=jnp.int32)
        rel = jax.nn.relu(jnp.einsum('bthd,bsd->bths', qib, ki).astype(jnp.float32) * (IDX_DIM ** -0.5))
        score = jnp.einsum('bths,bth->bts', rel, wib.astype(jnp.float32))
        causal = key_pos[None, :] <= t[:, None]
        score = jnp.where(causal[None], score, NEG)
        _, sel = lax.top_k(score, n_sel)
        valid = sel <= t[None, :, None]
        kg = jax.vmap(lambda a, i: a[i])(k, sel)
        vg = jax.vmap(lambda a, i: a[i])(v, sel)
        logit = jnp.einsum('bthd,btkhd->bhtk', qb, kg).astype(jnp.float32) * (B_HEAD_DIM ** -0.5)
        logit = jnp.where(valid[:, None], logit, NEG)
        p = jax.nn.softmax(logit, axis=-1).astype(vg.dtype)
        return jnp.einsum('bhtk,btkhd->bthd', p, vg)

    out = lax.map(block, (to_blocks(q), to_blocks(qi), to_blocks(wi), jnp.arange(nblk, dtype=jnp.int32)))
    return out.swapaxes(0, 1).reshape(bsz, s, B_WIDTH)

def short_gated_conv(cb, cc, cx, conv_w):
    z = cc * cx
    s = z.shape[1]
    zp = jnp.pad(z, ((0, 0), (CONV_WIDTH - 1, 0), (0, 0)))
    y = conv_w[0] * zp[:, 0:s]
    for i in range(1, CONV_WIDTH):
        y = y + conv_w[i] * zp[:, i:i + s]
    return cb * y

def token_mixers(h, positions, w_in, ws, bs, conv_w, w_proj_a, w_proj_b, w_proj_c, w_out):
    bsz, s, _ = h.shape
    proj = h @ w_in
    sizes = [A_WIDTH, A_WIDTH, B_WIDTH, B_WIDTH, B_WIDTH, IDX_HEADS * IDX_DIM, IDX_DIM, IDX_HEADS,
             C_WIDTH, C_WIDTH, C_WIDTH, N_BRANCH * D_MODEL]
    cuts = [int(c) for c in np.cumsum(sizes)[:-1]]
    u, va, q, k, vb, qi, ki, wi, cb, cc, cx, gates = jnp.split(proj, cuts, axis=-1)
    ya = gmlp_spatial(u, va, ws, bs)
    yb = dsa_attention(q, k, vb, qi, ki, wi, positions)
    yc = short_gated_conv(cb, cc, cx, conv_w)
    g = jax.nn.sigmoid(gates.astype(jnp.float32)).astype(h.dtype).reshape(bsz, s, N_BRANCH, D_MODEL)
    merged = g[:, :, 0] * (ya @ w_proj_a) + g[:, :, 1] * (yb @ w_proj_b) + g[:, :, 2] * (yc @ w_proj_c)
    return merged @ w_out

def hier_moe(h, rg_w, rg_b, re_w, re_b, w_gate, w_up, w_down):
    bsz, s, d = h.shape
    t_tok = bsz * s
    xt = h.reshape(t_tok, d)
    glog = (xt @ rg_w + rg_b).astype(jnp.float32)
    gprob = jax.nn.softmax(glog, axis=-1)
    grp = jnp.argmax(glog, axis=-1).astype(jnp.int32)
    gw = jnp.take_along_axis(gprob, grp[:, None], axis=1)[:, 0]
    elog = (xt @ re_w + re_b).astype(jnp.float32).reshape(t_tok, N_GROUPS, EXP_PER_GROUP)
    el = jnp.take_along_axis(elog, grp[:, None, None], axis=1)[:, 0]
    tv, ti = lax.top_k(el, TOP_K_EXP)
    tw = jax.nn.softmax(tv, axis=-1) * gw[:, None]
    n_assign = t_tok * TOP_K_EXP
    eid = (grp[:, None] * EXP_PER_GROUP + ti).reshape(n_assign)
    wts = tw.reshape(n_assign)
    tok = jnp.repeat(jnp.arange(t_tok, dtype=jnp.int32), TOP_K_EXP)
    order = jnp.argsort(eid)
    eid_s, wts_s, tok_s = eid[order], wts[order], tok[order]
    counts = jnp.bincount(eid, length=N_EXPERTS)
    start = jnp.cumsum(counts) - counts
    padded = ((counts + MOE_BLOCK - 1) // MOE_BLOCK) * MOE_BLOCK
    pend = jnp.cumsum(padded)
    pstart = pend - padded
    dest = pstart[eid_s] + (jnp.arange(n_assign, dtype=jnp.int32) - start[eid_s])
    n_blocks = -(-n_assign // MOE_BLOCK) + N_EXPERTS
    n_rows = n_blocks * MOE_BLOCK
    buf_tok = jnp.zeros((n_rows,), jnp.int32).at[dest].set(tok_s)
    buf_w = jnp.zeros((n_rows,), jnp.float32).at[dest].set(wts_s)
    block_exp = jnp.minimum(jnp.searchsorted(pend, jnp.arange(n_blocks, dtype=jnp.int32) * MOE_BLOCK, side='right'),
                            N_EXPERTS - 1).astype(jnp.int32)

    def expert_block(args):
        tok_b, e = args
        xb = xt[tok_b]
        hid = jax.nn.silu(xb @ w_gate[e]) * (xb @ w_up[e])
        return hid @ w_down[e]

    yb = lax.map(expert_block, (buf_tok.reshape(n_blocks, MOE_BLOCK), block_exp))
    yb = yb.reshape(n_rows, d) * buf_w[:, None].astype(xt.dtype)
    out = jnp.zeros((t_tok, d), xt.dtype).at[buf_tok].add(yb)
    return out.reshape(bsz, s, d)

def setup_inputs(seed: int = 0) -> dict:
    key = jax.random.key(seed)
    ks = jax.random.split(key, 20)
    f32 = jnp.float32
    nrm = lambda k, shape, scale: jax.random.normal(k, shape, f32) * scale
    return {
        "x": nrm(ks[0], (BATCH, SEQ, D_MODEL), 1.0),
        "positions": jnp.broadcast_to(jnp.arange(SEQ, dtype=jnp.int32), (BATCH, SEQ)),
        "norm_mix_g": 1.0 + nrm(ks[1], (DEPTH, D_MODEL), 0.02),
        "norm_ffn_g": 1.0 + nrm(ks[2], (DEPTH, D_MODEL), 0.02),
        "norm_final_g": 1.0 + nrm(ks[3], (D_MODEL,), 0.02),
        "w_in": nrm(ks[4], (DEPTH, D_MODEL, D_IN), D_MODEL ** -0.5),
        "gmlp_ws": nrm(ks[5], (DEPTH, A_GROUPS, CHUNK, CHUNK), CHUNK ** -0.5),
        "gmlp_b": 1.0 + nrm(ks[6], (DEPTH, A_GROUPS, CHUNK), 0.02),
        "conv_w": nrm(ks[7], (DEPTH, CONV_WIDTH, C_WIDTH), CONV_WIDTH ** -0.5),
        "w_proj_a": nrm(ks[8], (DEPTH, A_WIDTH, D_MODEL), A_WIDTH ** -0.5),
        "w_proj_b": nrm(ks[9], (DEPTH, B_WIDTH, D_MODEL), B_WIDTH ** -0.5),
        "w_proj_c": nrm(ks[10], (DEPTH, C_WIDTH, D_MODEL), C_WIDTH ** -0.5),
        "w_out": nrm(ks[11], (DEPTH, D_MODEL, D_MODEL), D_MODEL ** -0.5),
        "router_group_w": nrm(ks[12], (DEPTH, D_MODEL, N_GROUPS), D_MODEL ** -0.5),
        "router_group_b": nrm(ks[13], (DEPTH, N_GROUPS), 0.01),
        "router_expert_w": nrm(ks[14], (DEPTH, D_MODEL, N_EXPERTS), D_MODEL ** -0.5),
        "router_expert_b": nrm(ks[15], (DEPTH, N_EXPERTS), 0.01),
        "expert_w_gate": nrm(ks[16], (DEPTH, N_EXPERTS, D_MODEL, D_FF_EXPERT), D_MODEL ** -0.5),
        "expert_w_up": nrm(ks[17], (DEPTH, N_EXPERTS, D_MODEL, D_FF_EXPERT), D_MODEL ** -0.5),
        "expert_w_down": nrm(ks[18], (DEPTH, N_EXPERTS, D_FF_EXPERT, D_MODEL), D_FF_EXPERT ** -0.5),
    }

def reference(x, positions, norm_mix_g, norm_ffn_g, norm_final_g, w_in, gmlp_ws, gmlp_b, conv_w,
              w_proj_a, w_proj_b, w_proj_c, w_out, router_group_w, router_group_b,
              router_expert_w, router_expert_b, expert_w_gate, expert_w_up, expert_w_down):
    for l in range(DEPTH):
        h = rms_norm(x, norm_mix_g[l])
        x = x + token_mixers(h, positions, w_in[l], gmlp_ws[l], gmlp_b[l], conv_w[l],
                             w_proj_a[l], w_proj_b[l], w_proj_c[l], w_out[l])
        h = rms_norm(x, norm_ffn_g[l])
        x = x + hier_moe(h, router_group_w[l], router_group_b[l], router_expert_w[l], router_expert_b[l],
                         expert_w_gate[l], expert_w_up[l], expert_w_down[l])
    return rms_norm(x, norm_final_g)


_drawn_inputs = setup_inputs


def setup_inputs(seed=0):
    import zlib

    import numpy as np

    out = dict(_drawn_inputs(seed))
    spreads = {}
    factors = {'norm_final_g': 3.0, 'gmlp_b': 3.575, 'router_group_b': 6.879, 'router_expert_b': 5.078}
    for name, (base, spread) in spreads.items():
        noise = np.random.default_rng([zlib.crc32(name.encode()), seed]).standard_normal(out[name].shape)
        drawn = base * np.exp(spread * noise) if base else spread * noise
        out[name] = __import__('jax').numpy.asarray(drawn.astype(out[name].dtype))
    for name, factor in factors.items():
        out[name] = (out[name] * factor).astype(out[name].dtype)
    return out
```

```python
from contextlib import ExitStack

import numpy as np

import concourse.bass as bass
from concourse import mybir

P = 128
ALU = mybir.AluOpType
ACT = mybir.ActivationFunctionType
AX = mybir.AxisListType
F32 = mybir.dt.float32
F32R = mybir.dt.float32r
I32 = mybir.dt.int32
U32 = mybir.dt.uint32

ROPE_THETA = 500000.0
EPS = 1e-6
NEG = -1e30
TAKEN = -3e38
TWO_PI = 2.0 * np.pi
TWO_PI_HI = 6.28125
TWO_PI_MID = float(np.float32((TWO_PI - TWO_PI_HI) * 2**20 // 1 / 2**20))
TWO_PI_LO = TWO_PI - TWO_PI_HI - TWO_PI_MID
ROUND_MAGIC = 1.5 * 2.0**23


def build_trunk(nc, x_in, positions, norm_mix_g, norm_ffn_g, norm_final_g, w_in, gmlp_ws, gmlp_b, conv_w,
                w_proj_a, w_proj_b, w_proj_c, w_out, router_group_w, router_group_b,
                router_expert_w, router_expert_b, expert_w_gate, expert_w_up, expert_w_down, out):
    _, S, D = x_in.shape
    DEPTH, _, D_IN = w_in.shape
    NT = S // P
    KC = D // P
    HEADS, HD = 4, P
    WB = HEADS * HD
    IH, IDIM = 4, 64
    ROT = HD // 4 // 2
    IROT = IDIM // 4 // 2
    TOPK = min(256, S // 4)
    CONV = conv_w.shape[1]
    NG = router_group_w.shape[2]
    NE = router_expert_w.shape[2]
    EPG = NE // NG
    FF = expert_w_gate.shape[3]
    FC = FF // P
    BLK = 64
    QB = P // BLK
    MAIN_QUADS = NE // QB
    OVER_BLOCKS = (2 * S) // BLK
    TAB_BLOCKS = OVER_BLOCKS + QB
    MAX_QUADS = MAIN_QUADS + OVER_BLOCKS // QB
    assert (S, D, NT, KC, FC) == (256, 1024, 2, 8, 4) and TOPK % 8 == 0 and TOPK <= P
    LOGIT_SCALE = float(HD) ** -0.5
    IDX_SCALE = float(IDIM) ** -0.5
    IDX_W_SCALE = float(IH) ** -0.5
    N_ROUTE = NG + NE

    C_U, C_VA = 0, WB
    C_Q, C_K, C_V = 2 * WB, 3 * WB, 4 * WB
    C_QI = 5 * WB
    N_IDX = IH * IDIM + IDIM + IH
    C_CB = C_QI + N_IDX
    C_CC, C_CX = C_CB + WB, C_CB + 2 * WB
    C_GATE = C_CB + 3 * WB
    assert C_GATE + 3 * D == D_IN

    SLOTS = 12
    SLOT = 2048
    GROUPS = [C_QI, C_Q, C_K, C_V, C_VA, C_U, C_CX, C_CC, C_CB] + [C_GATE + WB * i for i in range(6)]
    G_QI, G_Q, G_K, G_V, G_VA, G_U, G_CX, G_CC, G_CB, G_GATE0 = range(10)
    N_IN = len(GROUPS)
    N_PROJ = 6
    MIX_SLOTS = 2 * N_IN + N_PROJ + 4
    MIX_RING = 7
    HIGHS = 4
    LOW_X = MIX_RING + HIGHS
    assert LOW_X == SLOTS - 1
    MIX_SPAN = -(-MIX_SLOTS // MIX_RING) * MIX_RING
    PAD = MIX_SPAN - MIX_SLOTS
    QUAD_SLOTS = 6 * QB
    STAGES = 6
    assert QUAD_SLOTS == SLOTS
    N_RESULTS = N_IN + N_PROJ + 2
    MIX_USES = [sum(1 for p in range(PAD, MIX_SPAN) if p % MIX_RING == s) if s < MIX_RING else 0 for s in range(SLOTS)]
    P_OUT = {(part, half): MIX_SPAN - 4 + 2 * part + half for part in range(2) for half in range(2)}

    def result_of(p):
        i = p - PAD
        if i < 2 * N_IN:
            return i // 2 + 1
        i -= 2 * N_IN
        return N_IN + 1 + (i if i < N_PROJ else N_PROJ + (i - N_PROJ) % 2)

    def mixing_reader(s):
        if s < MIX_RING:
            return result_of(MIX_SPAN - MIX_RING + s)
        if s == LOW_X:
            return N_IN
        return max(result_of(p) for p in range(MIX_SPAN - HIGHS, MIX_SPAN) if p % HIGHS == s - MIX_RING)

    def words_of(p):
        return 4 * N_IDX if (p - PAD) // 2 == G_QI else SLOT

    DVE_MIX = 117

    with ExitStack() as ctx:
        place = {}

        def sb(name, shape, dt=F32):
            place[name] = -(-nc.sbuf_base // 32) * 32, shape
            return ctx.enter_context(nc.sbuf_tensor(name, shape, dt))

        def rounded(name):
            offset, shape = place[name]
            return nc.alloc_sbuf_tensor_at(name + "_parts", shape, F32R, offset=offset)

        def psum(name):
            return ctx.enter_context(nc.psum_tensor(name, [P, 2, 512], F32))

        def sem(name):
            return ctx.enter_context(nc.semaphore(name))

        psA, psB, psC, psD = psum("psA"), psum("psB"), psum("psC"), psum("psD")

        ring = sb("ring", [P, SLOTS, SLOT])
        x = sb("x", [P, NT, D])
        xn = sb("xn", [P, NT * D])
        hT = sb("hT", [P, KC, S])
        share1 = sb("share1", [P, 2048])
        gates = sb("gates", [P, 6, 4, S])
        idx = sb("idx", [P, NT, 3 * P + IH])
        qiT = sb("qiT", [P, 2, S])
        kiT = sb("kiT", [P, S])
        rel = sb("rel", [P, HEADS, S])
        p0 = sb("p0", [P, HEADS, P])
        score = sb("score", [P, S])
        work = sb("work", [P, S])
        maskb = sb("maskb", [P, NT, S])
        ybT = sb("ybT", [P, HEADS, S], F32R)        
        vg = sb("vg", [P, NT, WB])
        uT = sb("uT", [P, HEADS, S])
        wsT = sb("wsT", [P, HEADS, P])
        bs_row = sb("bs_row", [1, WB])
        z = sb("z", [P, 4, S + CONV - 1])
        ycT = sb("ycT", [P, 4, S])
        tmp = sb("tmp", [P, 1024])
        rope_tmp = tmp[:, 0:4 * NT * HEADS * ROT]

        q_tok = share1[:, 0:1024].rearrange("p (t n) -> p t n", t=NT)
        k_tok = share1[:, 1024:2048].rearrange("p (t n) -> p t n", t=NT)
        merged = share1[:, :].rearrange("p (c s) -> p c s", c=KC)
        qT = xn[:, 0:1024].rearrange("p (h s) -> p h s", h=HEADS)
        kT = xn[:, 1024:2048].rearrange("p (h s) -> p h s", h=HEADS)
        v_tok = gates[:, 5].rearrange("p m s -> p (m s)").rearrange("p (t n) -> p t n", t=NT)
        pT = gates[:, 3:5].rearrange("p g m s -> p (g m s)")[:, 0:3 * WB].rearrange(
            "p (k h q) -> p k h q", k=3, h=HEADS)
        ws_raw = gates[:, 2].rearrange("p m s -> p (m s)")[:, 0:WB].rearrange("p (h s) -> p h s", h=HEADS)
        ring_parts = rounded("ring")
        hT_low = ring_parts[:, LOW_X, :].rearrange("p (c s) -> p c s", c=KC)
        hT_high = rounded("hT")
        merged_high, merged_low = hT_high, rounded("share1")[:, :].rearrange("p (c s) -> p c s", c=KC)
        xn_parts = rounded("xn")
        ya_high, yb_low = [xn_parts[:, i * 1024:(i + 1) * 1024].rearrange("p (c s) -> p c s", c=4) for i in range(2)]
        branch_high = (ya_high, ybT, rounded("rel"))
        branch_low = (rounded("uT"), yb_low, rounded("ycT"))
        xT = share1[:, 0:1024].rearrange("p (c n) -> p c n", c=KC)
        hidT = share1[:, 1024:1536].rearrange("p (c n) -> p c n", c=FC)
        hid = share1[:, 1536:2048]
        y = gates[:, 0].rearrange("p m s -> p (m s)").rearrange("p (n w) -> p n w", n=2)
        silu = gates[:, 1].rearrange("p m s -> p (m s)")[:, 0:512]
        selwT = gates[:, 1].rearrange("p m s -> p (m s)")[:, 512:768].rearrange("p (t n) -> p t n", t=NT)
        sel = gates[:, 2].rearrange("p m s -> p (m s)")[:, 0:256].rearrange("p (t j n) -> p t j n", t=NT, j=QB)
        selw = gates[:, 2].rearrange("p m s -> p (m s)")[:, 256:512].rearrange("p (t j n) -> p t j n", t=NT, j=QB)
        over1 = rel[:, 0:2].rearrange("p h s -> p (h s)")[:, 0:TAB_BLOCKS * NE].rearrange("p (b e) -> p b e", e=NE)
        over2 = rel[:, 2:4].rearrange("p h s -> p (h s)")[:, 0:TAB_BLOCKS * NE].rearrange("p (b e) -> p b e", e=NE)
        gfin = tmp

        ident = sb("ident", [P, P])
        before = sb("before", [P, P])
        ones = sb("ones", [P, P])
        causal = sb("causal", [P, S])
        iota = sb("iota", [P, BLK])
        thresholds = sb("thresholds", [P, S // BLK - 1])
        rows = sb("rows", [DEPTH * (KC + CONV * 4), P])
        cols = sb("cols", [P, DEPTH * (KC + CONV * 4)])
        g_mix = sb("g_mix", [P, KC])
        w_conv = sb("w_conv", [P, CONV * 4])
        g_ffn_all = sb("g_ffn_all", [P, DEPTH, KC])
        g_ffn = sb("g_ffn", [P, KC])
        rg_all = sb("rg_all", [P, DEPTH, KC, NG])
        re_all = sb("re_all", [P, DEPTH, KC, NE])
        rgb_all = sb("rgb_all", [P, DEPTH, NG])
        reb_all = sb("reb_all", [P, DEPTH, NE])
        r_w = sb("r_w", [P, KC, N_ROUTE])
        r_b = sb("r_b", [P, N_ROUTE])
        pos_i = sb("pos_i", [P, NT], I32)
        pos_f = sb("pos_f", [P, NT])
        inv_freq = sb("inv_freq", [P, ROT])
        ang = sb("ang", [P, 3, NT, ROT])
        cos = sb("cos", [P, NT, ROT])
        sin = sb("sin", [P, NT, ROT])

        ss = sb("ss", [P, NT])
        var = sb("var", [P, NT])
        inv = sb("inv", [P, NT])
        rstd = sb("rstd", [P, NT])
        newton = sb("newton", [P, NT])
        stats = sb("stats", [P, NT, 6])
        mv = sb("mv", [P, NT, 2])
        wi = sb("wi", [P, NT, IH])
        top8 = sb("top8", [P, 8])
        mx = sb("mx", [P, NT, HEADS])
        den = sb("den", [P, NT, HEADS])
        rden = sb("rden", [P, NT, HEADS])

        glog = sb("glog", [P, NT, 8])
        gtop = sb("gtop", [P, NT, 8])
        gtop_i = sb("gtop_i", [P, NT, 8], U32)
        gidx = sb("gidx", [P, NT])
        goh = sb("goh", [P, NT, NG])
        gpen = sb("gpen", [P, NT, NG])
        etop = sb("etop", [P, NT, 8])
        etop_i = sb("etop_i", [P, NT, 8], U32)
        eidx = sb("eidx", [P, NT, 2])
        ex = sb("ex", [P, NT, NG + 1])
        tw = sb("tw", [P, NT, 2])
        gsum = sb("gsum", [P, NT])
        NBL = NE + TAB_BLOCKS
        routing = ycT[:, :, :].rearrange("p m s -> p (m s)")
        taken = [0]

        def part(n):
            taken[0] += n
            return routing[:, taken[0] - n:taken[0]]

        elog = part(NT * NE).rearrange("p (t g e) -> p t g e", t=NT, g=NG)
        em = part(NT * NE).rearrange("p (t g e) -> p t g e", t=NT, g=NG)
        oh0 = part(NT * NE).rearrange("p (t e) -> p t e", t=NT)
        oh1 = part(NT * NE).rearrange("p (t e) -> p t e", t=NT)
        member = part(NT * NE).rearrange("p (t e) -> p t e", t=NT)
        beyond = part(NE * (S // BLK - 1)).rearrange("p (e k) -> p e k", e=NE)
        pos_tab = part(NT * NBL).rearrange("p (t b) -> p t b", t=NT)
        wt_tab = part(NT * NBL).rearrange("p (t b) -> p t b", t=NT)
        cumA = sb("cumA", [P, 16 + NE])
        cumB = sb("cumB", [P, 16 + NE])
        total = sb("total", [P, 1])
        credit = sb("credit", [P, STAGES])
        nquad = sb("nquad", [P, OVER_BLOCKS // QB])
        quads_f = sb("quads_f", [P, 1])
        quads_i = sb("quads_i", [P, DEPTH + 1], I32)
        over_e = sb("over_e", [P, TAB_BLOCKS])
        over_prev = sb("over_prev", [P, TAB_BLOCKS])
        over_i = sb("over_i", [P, TAB_BLOCKS], I32)
        over_r = sb("over_r", [P, TAB_BLOCKS])
        bidx = sb("bidx", [P, TAB_BLOCKS])

        landed = [sem(f"landed{s}") for s in range(SLOTS)]
        x_landed = sem("x_landed")
        small_landed = sem("small_landed")
        ws_landed = sem("ws_landed")
        gfin_landed = sem("gfin_landed")
        out_stored = sem("out_stored")

        zeroed = sem("zeroed")
        consts = sem("consts")
        passed = sem("passed")
        tri_done = sem("tri_done")
        quad_freed = sem("quad_freed")

        cols_ps = sem("cols_ps")
        hT_ps = sem("hT_ps")
        mixed = sem("mixed")
        idxT_ps = sem("idxT_ps")
        score_ps = sem("score_ps")
        qT_ps = sem("qT_ps")
        kT_ps = sem("kT_ps")
        logit_ps = sem("logit_ps")
        pT_ps = sem("pT_ps")
        ybT_ps = sem("ybT_ps")
        wsT_ps = sem("wsT_ps")
        vm_ps = sem("vm_ps")
        route_ps = sem("route_ps")
        rank_ps = sem("rank_ps")
        gather_ps = sem("gather_ps")
        selT_ps = sem("selT_ps")
        hidT_ps = sem("hidT_ps")
        scatter_ps = [sem(f"scatter_ps{t}") for t in range(NT)]

        ss_act = sem("ss_act")
        root = sem("root")
        xn_act = sem("xn_act")
        hT_act = sem("hT_act")
        high_act = sem("high_act")
        branch_act = sem("branch_act")
        merged_act = sem("merged_act")
        act_out = sem("act_out")
        idxT_act = sem("idxT_act")
        rel_act = sem("rel_act")
        qT_act = sem("qT_act")
        kT_act = sem("kT_act")
        exp_act = sem("exp_act")
        pT_act = sem("pT_act")
        ybT_act = sem("ybT_act")
        wsT_act = sem("wsT_act")
        route_exp = sem("route_exp")
        trig_act = sem("trig_act")
        selT_act = sem("selT_act")
        silu_act = sem("silu_act")
        hidT_act = sem("hidT_act")
        y_act = sem("y_act")

        setup_link = sem("setup_link")
        dve_link = sem("dve_link")
        quad_link = sem("quad_link")
        setup_done = sem("setup_done")
        layer_cols = sem("layer_cols")
        inv_dve = sem("inv_dve")
        rstd_dve = sem("rstd_dve")
        xn_dve = sem("xn_dve")
        hT_dve = sem("hT_dve")
        low_dve = sem("low_dve")
        branch_low_dve = sem("branch_low_dve")
        merged_low_dve = sem("merged_low_dve")
        dve_out = sem("dve_out")
        idx_roped = sem("idx_roped")
        q_roped = sem("q_roped")
        k_roped = sem("k_roped")
        score_dve = sem("score_dve")
        exp_args = sem("exp_args")
        probs = sem("probs")
        v_normed = sem("v_normed")
        yaT_done = sem("yaT_done")
        ycT_done = sem("ycT_done")
        merged_done = sem("merged_done")
        route_args = sem("route_args")
        members = sem("members")
        quads_known = sem("quads_known")
        over_known = sem("over_known")
        sel_done = sem("sel_done")
        xT_done = sem("xT_done")
        hid_done = sem("hid_done")
        y_dve = sem("y_dve")
        x_added = sem("x_added")
        final_done = sem("final_done")

        on_act = [n for n in range(N_RESULTS) if n <= G_U or G_GATE0 <= n < N_IN]
        on_dve = [n for n in range(N_RESULTS) if n not in on_act]
        N_SETUP = 10

        block = ctx.enter_context(nc.Block())

        def alone(eng):
            eng.sem_inc(passed)

        def slot(s, n):
            return ring[:, s % SLOTS, 0:n]

        def unit_slots(unit):
            return [PAD + 2 * unit, PAD + 2 * unit + 1]

        def high_and_low(p):
            return [ring_parts[:, s, 0:words_of(p)] for s in (MIX_RING + p % HIGHS, p % MIX_RING)]

        def mix_slot(p):
            return ring[:, p % MIX_RING, 0:words_of(p)]


        def sync_program(sp):
            for t in range(NT):
                sp.dma_start(x[:, t, :], x_in[0, t * P:(t + 1) * P, :]).then_inc(x_landed, 16)
            small_loads(sp)
            with sp.Fori(0, DEPTH) as l:
                if_known = l * 1 + 1
                sp.wait_ge(quads_known, if_known)
                alone(sp)
                done = sp.value_load(quads_i[0:1, bass.ds(l, 1)], min_val=0, max_val=DEPTH * MAX_QUADS)

                def load(src, s, words):
                    dst = ring[:, s, 0:words]
                    if len(src.shape) == 3:
                        dst = dst.rearrange("p (c n) -> p c n", c=src.shape[1])
                    sp.dma_start(dst, src).then_inc(landed[s], 16)

                for p in range(PAD, MIX_SPAN):
                    if p - MIX_RING >= PAD:
                        sp.wait_ge(mixed, l * N_RESULTS + result_of(p - MIX_RING))
                    else:
                        sp.wait_ge(quad_freed, done * STAGES + 1 + (p % MIX_RING) // QB)
                    alone(sp)
                    i = p - PAD
                    if i < 2 * N_IN:
                        g, half = i // 2, i % 2
                        n = N_IDX if g == G_QI else WB
                        src = w_in.rearrange("l (c p) n -> l p c n", p=P)[
                            bass.ds(l, 1), :, 4 * half:4 * half + 4, GROUPS[g]:GROUPS[g] + n]
                    elif i < 2 * N_IN + N_PROJ:
                        k = i - 2 * N_IN
                        w, half = (w_proj_a, w_proj_b, w_proj_c)[k % 3], k // 3
                        n = 512
                        src = w.rearrange("l (c p) n -> l p c n", p=P)[bass.ds(l, 1), :, :, 512 * half:512 * half + 512]
                    else:
                        part, half = (i - 2 * N_IN - N_PROJ) // 2, i % 2
                        assert P_OUT[part, half] == p
                        n = 512
                        src = w_out.rearrange("l (c p) n -> l p c n", p=P)[
                            bass.ds(l, 1), :, 4 * part:4 * part + 4, 512 * half:512 * half + 512]
                    load(src.rearrange("l p c n -> p (l c) n"), p % MIX_RING, 4 * n)
                    if i == 2 * G_CX:
                        sp.dma_start(ws_raw[:, :, :], gmlp_ws.rearrange("l g t s -> l t g s")[
                            bass.ds(l, 1)].rearrange("l t g s -> t (l g) s")).then_inc(ws_landed, 16)
                        sp.dma_start(bs_row[0:1, :], gmlp_b.rearrange("l g t -> l (g t)")[
                            bass.ds(l, 1)]).then_inc(ws_landed, 16)

                def load_quad(g, experts):
                    for p in range(QUAD_SLOTS):
                        k, j = p // QB, p % QB
                        if j == 0:
                            sp.wait_ge(mixed, l * N_RESULTS + max(mixing_reader(p + i) for i in range(QB)))
                            alone(sp)
                            sp.wait_ge(quad_freed, g * STAGES + 1 + k)
                            alone(sp)
                        e = experts[j]
                        if k < 4:
                            w = (expert_w_gate, expert_w_up)[k % 2]
                            src = w.rearrange("l e (p c) n -> (l e) p (c n)", c=KC)[
                                bass.ds(e, 1), :, SLOT * (k // 2):SLOT * (k // 2 + 1)]
                        else:
                            src = expert_w_down.rearrange("l e (p c) n -> (l e) p (c n)", c=FC)[
                                bass.ds(e, 1), :, SLOT * (k - 4):SLOT * (k - 3)]
                        load(src.rearrange("e p n -> (e p) n"), p, SLOT)

                with sp.Fori(0, MAIN_QUADS) as i:
                    load_quad(done + i, [l * NE + i * QB + j for j in range(QB)])
                sp.wait_ge(quads_known, l + 2)
                sp.wait_ge(over_known, l + 1)
                alone(sp)
                end = sp.value_load(quads_i[0:1, bass.ds(l + 1, 1)], min_val=MAIN_QUADS, max_val=DEPTH * MAX_QUADS)
                with sp.If(end > done + MAIN_QUADS):
                    with sp.Fori(0, nc.s_assert_within(end - done - MAIN_QUADS, 0, OVER_BLOCKS // QB)) as i:
                        experts = [sp.value_load(over_i[0:1, bass.ds(i * QB + j, 1)], min_val=0, max_val=NE - 1)
                                   for j in range(QB)]
                        load_quad(done + MAIN_QUADS + i, [l * NE + e for e in experts])
            sp.wait_ge(merged_done, 2 * DEPTH)
            sp.dma_start(gfin[:, :], norm_final_g.rearrange("(a d) -> a d", a=1).to_broadcast([P, D])).then_inc(gfin_landed, 16)
            for t in range(NT):
                sp.wait_ge(final_done, t + 1)
                sp.dma_start(out[0, t * P:(t + 1) * P, :], xn[:, t * D:(t + 1) * D]).then_inc(out_stored, 16)
            sp.wait_ge(out_stored, 16 * NT)

        def small_loads(sp):
            with nc.allow_non_contiguous_dma(reason="256 positions and a few gains"):
                sp.dma_start(rows[0:DEPTH * KC, :], norm_mix_g.rearrange("l (c p) -> (l c) p", p=P)).then_inc(small_landed, 16)
                sp.dma_start(rows[DEPTH * KC:, :], conv_w.rearrange("l k (c p) -> (l k c) p", p=P)).then_inc(small_landed, 16)
                sp.dma_start(pos_i[:, :], positions.rearrange("a (t p) -> p (a t)", p=P)).then_inc(small_landed, 16)
                sp.dma_start(g_ffn_all[:, :, :], norm_ffn_g.rearrange("l (p c) -> p l c", c=KC)).then_inc(small_landed, 16)
                sp.dma_start(rg_all[:, :, :, :].rearrange("p l c n -> p l (c n)"),
                             router_group_w.rearrange("l (p c) n -> p l (c n)", c=KC)).then_inc(small_landed, 16)
                sp.dma_start(re_all[:, :, :, :].rearrange("p l c n -> p l (c n)"),
                             router_expert_w.rearrange("l (p c) n -> p l (c n)", c=KC)).then_inc(small_landed, 16)
                sp.dma_start(rgb_all[:, :, :].rearrange("p l n -> p (l n)"),
                             router_group_b.rearrange("(a l) n -> a (l n)", a=1).to_broadcast([P, DEPTH * NG])).then_inc(small_landed, 16)
                sp.dma_start(reb_all[:, :, :].rearrange("p l n -> p (l n)"),
                             router_expert_b.rearrange("(a l) n -> a (l n)", a=1).to_broadcast([P, DEPTH * NE])).then_inc(small_landed, 16)
        N_SMALL = 8

        def pool_program(pool):
            gp = nc.gpsimd
            gp.memset(ident[:, :], 0.0).then_inc(zeroed, 1)
            gp.memset(before[:, :], 0.0).then_inc(zeroed, 1)
            gp.memset(causal[:, :], 0.0).then_inc(zeroed, 1)
            gp.memset(ones[:, :], 1.0)
            gp.memset(z[:, :, :], 0.0)
            gp.memset(cumA[:, :], 0.0)
            gp.memset(cumB[:, :], 0.0)
            gp.memset(glog[:, :, :], TAKEN)
            for j in range(ROT):
                gp.memset(inv_freq[:, j:j + 1], float(np.float32(ROPE_THETA) ** np.float32(-j * 2.0 / (2 * ROT))))
            gp.iota(iota[:, :], pattern=[[1, BLK]], base=0, channel_multiplier=0, allow_small_or_imprecise_dtypes=True)
            gp.iota(bidx[:, :], pattern=[[1, TAB_BLOCKS]], base=0, channel_multiplier=0, allow_small_or_imprecise_dtypes=True)
            gp.iota(thresholds[:, :], pattern=[[BLK, S // BLK - 1]], base=BLK, channel_multiplier=0, allow_small_or_imprecise_dtypes=True)
            pool.wait_ge(zeroed, 3)
            gp.affine_select(out=ident[:, :], in_=ident[:, :], compare_op=ALU.not_equal, fill=1.0, base=0,
                             pattern=[[-1, P]], channel_multiplier=1).then_inc(consts, 1)
            gp.affine_select(out=before[:, :], in_=before[:, :], compare_op=ALU.is_ge, fill=1.0, base=0,
                             pattern=[[-1, P]], channel_multiplier=1).then_inc(consts, 1)
            gp.affine_select(out=causal[:, :], in_=causal[:, :], compare_op=ALU.is_ge, fill=NEG, base=P,
                             pattern=[[-1, S]], channel_multiplier=1).then_inc(consts, 1)
            for k in range(STAGES):
                gp.memset(credit[:, k:k + 1], 0.0).then_inc(quad_freed, 1)
            with pool.Fori(0, DEPTH) as l:
                pool.wait_ge(wsT_act, l + 1)
                alone(pool)
                gp.affine_select(out=wsT[:, :, :], in_=wsT[:, :, :], compare_op=ALU.is_ge, fill=0.0, base=0,
                                 pattern=[[0, HEADS], [1, P]], channel_multiplier=-1).then_inc(tri_done, 1)

        def scalar_program(act):
            sc = nc.scalar
            act.wait_ge(setup_link, TRIG_READY)
            sc.activation(sin[:, :, :], ang[:, 0], ACT.Sin)
            sc.activation(cos[:, :, :], ang[:, 1], ACT.Sin).then_inc(trig_act, 1)
            with act.Fori(0, DEPTH) as l:
                act.wait_ge(quads_known, l + 1)
                alone(act)
                start = act.value_load(quads_i[0:1, bass.ds(l, 1)], min_val=0, max_val=DEPTH * MAX_QUADS)

                def norm(which, gain, permuted):
                    if which == 0:
                        act.wait_ge(x_landed, 16 * NT)
                        act.wait_ge(x_added, start * 2 + 1)
                    else:
                        act.wait_ge(dve_out, (l + 1) * len(on_dve))
                    sc.activation(xn[:, 0:D], x[:, 0, :], ACT.Square, accum_out=ss[:, 0:1]).then_inc(ss_act, 1)
                    root_of(2 * which)
                    act.wait_ge(rstd_dve, l * 2 + which + 1)
                    dst = xn[:, 0:D]
                    src = x[:, 0, :]
                    if permuted:
                        dst = dst.rearrange("p (c q) -> p c q", c=KC)
                        src = src.rearrange("p (q c) -> p c q", c=KC)
                    sc.activation(dst, src, ACT.Copy, scale=rstd[:, 0:1]).then_inc(xn_act, 1)
                    if which == 0:
                        high(*unit_slots(0))
                    act.wait_ge(layer_cols, l + 1)
                    dst = hT_high if which == 0 else hT
                    for b in range(4) if which == 0 else (0, 2):
                        act.wait_ge(hT_ps, l * 8 + which * 4 + b + 1)
                        for c in range(2):
                            ins = sc.activation(dst[:, 2 * b + c, :], (psA, psB)[b // 2][:, b % 2, c * S:(c + 1) * S], ACT.Copy,
                                                scale=gain[:, 2 * b + c:2 * b + c + 1])
                        ins.then_inc(hT_act, 1)

                def high(*ps):
                    for p in ps:
                        s = p % MIX_RING
                        k = sum(1 for q in range(PAD, p + 1) if q % MIX_RING == s)
                        act.wait_ge(landed[s], l * (16 * MIX_USES[s]) + start * 16 + 16 * k)
                        if p - HIGHS >= PAD:
                            act.wait_ge(mixed, l * N_RESULTS + result_of(p - HIGHS))
                        sc.activation(high_and_low(p)[0], mix_slot(p), ACT.Copy).then_inc(high_act, 1)

                def root_of(n):
                    act.wait_ge(inv_dve, l * 3 + n + 1)
                    sc.activation(rstd[:, :], inv[:, :], ACT.Sqrt).then_inc(root, 1)

                def merged_part(half):
                    act.wait_ge(merged_done, l * 2 + half + 1)
                    sc.activation(merged_high[:, 4 * half:4 * half + 4, :], merged[:, 4 * half:4 * half + 4, :],
                                  ACT.Copy).then_inc(merged_act, 1)

                def result(n):
                    act.wait_ge(mixed, l * N_RESULTS + n + 1)
                    return (psA, psB)[n % 2]

                norm(0, g_mix, False)
                high(*unit_slots(1))
                ps = result(G_QI)
                sc.activation(idx[:, :, 0:320], ps[:, :, 0:320], ACT.Copy)
                sc.activation(idx[:, :, 384:388], ps[:, :, 320:324], ACT.Copy).then_inc(act_out, 1)
                high(*unit_slots(2))
                sc.activation(q_tok, result(G_Q)[:, :, :], ACT.Copy).then_inc(act_out, 1)
                act.wait_ge(idxT_ps, l + 1)
                sc.activation(qiT[:, :, :], psC[:, 0, :].rearrange("p (a s) -> p a s", a=2), ACT.Copy)
                sc.activation(kiT[:, :], psC[:, 1, 0:S], ACT.Copy).then_inc(idxT_act, 1)
                high(*unit_slots(3))
                sc.activation(k_tok, result(G_K)[:, :, :], ACT.Copy).then_inc(act_out, 1)
                high(unit_slots(4)[0])
                act.wait_ge(score_ps, l * 2 + 1)
                for r in range(2):
                    ins = sc.activation(p0[:, r::2, :], psD[:, r, 0:S].rearrange("p (a s) -> p a s", a=2), ACT.Relu, scale=IDX_SCALE)
                ins.then_inc(rel_act, 1)
                act.wait_ge(score_ps, l * 2 + 2)
                for r in range(2):
                    ins = sc.activation(rel[:, r::2, :], psC[:, r, :].rearrange("p (a s) -> p a s", a=2), ACT.Relu, scale=IDX_SCALE)
                ins.then_inc(rel_act, 1)
                high(unit_slots(4)[1])
                sc.activation(v_tok, result(G_V)[:, :, :], ACT.Copy).then_inc(act_out, 1)
                high(*unit_slots(5))
                act.wait_ge(qT_ps, l + 1)
                sc.activation(qT.rearrange("p (b h) s -> p b (h s)", b=2), psD[:, :, :], ACT.Copy).then_inc(qT_act, 1)
                sc.activation(vg[:, :, :], result(G_VA)[:, :, :], ACT.Gelu_apprx_tanh).then_inc(act_out, 1)
                high(*unit_slots(6))
                act.wait_ge(kT_ps, l + 1)
                sc.activation(kT.rearrange("p (b h) s -> p b (h s)", b=2), psC[:, :, :], ACT.Copy).then_inc(kT_act, 1)
                sc.activation(uT[:, :, :].rearrange("p (b h) s -> p b (h s)", b=2), result(G_U)[:, :, :],
                              ACT.Gelu_apprx_tanh).then_inc(act_out, 1)
                high(*unit_slots(7))
                for b, pr, nk in ((0, p0, P), (1, rel, S)):
                    act.wait_ge(exp_args, l * 2 + b + 1)
                    for h in range(HEADS):
                        ins = sc.activation(pr[:, h, 0:nk], pr[:, h, 0:nk], ACT.Exp, bias=mx[:, b, h:h + 1],
                                            accum_out=den[:, b, h:h + 1])
                    ins.then_inc(exp_act, 1)
                root_of(1)
                high(*unit_slots(8))
                high(*unit_slots(9))
                act.wait_ge(pT_ps, l * 2 + 2)
                sc.activation(pT[:, 0, :, :].rearrange("p h q -> p (h q)"), psD[:, 1, :], ACT.Copy)
                sc.activation(pT[:, 1:3, :, :].rearrange("p k h q -> p k (h q)"), psC[:, :, :], ACT.Copy).then_inc(pT_act, 1)
                high(*unit_slots(10))
                act.wait_ge(ybT_ps, l + 1)
                sc.activation(ybT[:, :, :].rearrange("p (b h) s -> p b (h s)", b=2), psD[:, :, :], ACT.Copy).then_inc(ybT_act, 1)
                act.wait_ge(wsT_ps, l + 1)
                sc.activation(wsT[:, :, :].rearrange("p h s -> p (h s)"), psC[:, 0, :], ACT.Copy).then_inc(wsT_act, 1)
                act.wait_ge(dve_out, l * len(on_dve) + 1 + on_dve.index(G_CB))
                sc.activation(branch_high[2][:, :, :], ycT[:, :, :], ACT.Copy).then_inc(branch_act, 1)
                for n in range(6):
                    sc.activation(gates[:, n].rearrange("p (b h) s -> p b (h s)", b=2), result(G_GATE0 + n)[:, :, :],
                                  ACT.Sigmoid).then_inc(act_out, 1)
                    if n == 2:
                        act.wait_ge(yaT_done, l + 1)
                        sc.activation(ya_high, uT[:, :, :], ACT.Copy).then_inc(branch_act, 1)
                    high(*unit_slots(G_GATE0 + n + 2))
                high(*unit_slots(17))
                merged_part(0)
                high(*unit_slots(18))
                high(*unit_slots(19))
                merged_part(1)

                norm(1, g_ffn, True)
                act.wait_ge(route_args, l + 1)
                sc.activation(ex[:, :, :], ex[:, :, :], ACT.Exp).then_inc(route_exp, 1)

                act.wait_ge(quads_known, l + 2)
                alone(act)
                end = act.value_load(quads_i[0:1, bass.ds(l + 1, 1)], min_val=MAIN_QUADS, max_val=DEPTH * MAX_QUADS)
                with act.Fori(start, end) as g:
                    act.wait_ge(selT_ps, g + 1)
                    sc.activation(selwT.rearrange("p t n -> p (t n)"), psD[:, 1, 0:S], ACT.Copy).then_inc(selT_act, 1)
                    act.wait_ge(quad_freed, g * STAGES + STAGES + 3)
                    sc.activation(silu, psB[:, 0, :], ACT.Silu).then_inc(silu_act, 1)
                    act.wait_ge(hidT_ps, g + 1)
                    sc.activation(hidT.rearrange("p c n -> p (c n)"), psD[:, 0, :], ACT.Copy).then_inc(hidT_act, 1)
                    act.wait_ge(quad_freed, g * STAGES + 2 * STAGES)
                    sc.activation(y[:, 0, :], psC[:, 0, :], ACT.Copy).then_inc(y_act, 1)

            act.wait_ge(quads_known, DEPTH + 1)
            last = act.value_load(quads_i[0:1, DEPTH:DEPTH + 1], min_val=MAIN_QUADS, max_val=DEPTH * MAX_QUADS)
            act.wait_ge(x_added, last * 2)
            sc.activation(xn[:, 0:D], x[:, 0, :], ACT.Square, accum_out=ss[:, 0:1]).then_inc(ss_act, 1)
            act.wait_ge(inv_dve, 3 * DEPTH + 1)
            sc.activation(rstd[:, :], inv[:, :], ACT.Sqrt).then_inc(root, 1)

        def vector_program(dve):
            v = nc.vector
            count = [0]

            def setup(ins):
                count[0] += 1
                ins.then_inc(setup_link, 1)
                dve.wait_ge(setup_link, count[0])

            setup(v.memset(quads_f[:, :], 0.0))
            v.memset(quads_i[:, :], 0).then_inc(quads_known, 1)
            v.memset(total[:, :], 0.0).then_inc(x_added, 1)
            dve.wait_ge(small_landed, 16 * N_SMALL)
            dve.wait_ge(consts, 3)
            setup(v.tensor_copy(pos_f[:, :], pos_i[:, :]))
            for t in range(NT):
                ins = v.tensor_scalar(ang[:, 2, t, :], inv_freq[:, :], pos_f[:, t:t + 1], None, ALU.mult)
            setup(ins)
            setup(v.tensor_scalar(ang[:, 1], ang[:, 2], 1.0 / TWO_PI, ROUND_MAGIC, ALU.mult, ALU.add))
            setup(v.tensor_scalar(ang[:, 1], ang[:, 1], ROUND_MAGIC, None, ALU.subtract))
            setup(v.scalar_tensor_tensor(ang[:, 2], ang[:, 1], -TWO_PI_HI, ang[:, 2], ALU.mult, ALU.add))
            setup(v.scalar_tensor_tensor(ang[:, 2], ang[:, 1], -TWO_PI_MID, ang[:, 2], ALU.mult, ALU.add))
            setup(v.scalar_tensor_tensor(ang[:, 2], ang[:, 1], -TWO_PI_LO, ang[:, 2], ALU.mult, ALU.add))
            lim = float(np.nextafter(np.float32(np.pi), np.float32(0)))
            setup(v.tensor_scalar(ang[:, 0], ang[:, 2], lim, -lim, ALU.min, ALU.max))
            setup(v.scalar_tensor_tensor(ang[:, 1], ang[:, 0], -1.0, ang[:, 0], ALU.mult, ALU.max))
            setup(v.tensor_scalar(ang[:, 1], ang[:, 1], -1.0, float(np.pi / 2), ALU.mult, ALU.add))
            assert count[0] == TRIG_READY
            dve.wait_ge(cols_ps, 1)
            v.tensor_copy(cols[:, :], psD[:, 1, 0:cols.shape[1]]).then_inc(setup_done, 1)
            dve.wait_ge(setup_done, 1)

            with dve.Fori(0, DEPTH) as l:
                linked = [0]

                def link(ins, wait_alone=False):
                    linked[0] += 1
                    ins.then_inc(dve_link, 1)
                    dve.wait_ge(dve_link, l * DVE_MIX + linked[0])
                    if wait_alone:
                        alone(dve)

                def rstd_from(src, scale, n):
                    link(v.tensor_scalar(var[:, :], src, scale, EPS, ALU.mult, ALU.add))
                    v.reciprocal(inv[:, :], var[:, :]).then_inc(inv_dve, 1)
                    return n

                def newton_step(n):
                    dve.wait_ge(root, l * 3 + n + 1)
                    link(v.tensor_tensor(newton[:, :], rstd[:, :], rstd[:, :], ALU.mult))
                    link(v.tensor_tensor(newton[:, :], newton[:, :], var[:, :], ALU.mult))
                    link(v.tensor_scalar(newton[:, :], newton[:, :], -0.5, 1.5, ALU.mult, ALU.add))
                    return v.tensor_tensor(rstd[:, :], rstd[:, :], newton[:, :], ALU.mult)

                def low(*ps):
                    for p in ps:
                        dve.wait_ge(high_act, l * MIX_SLOTS + p - PAD + 1)
                        high_part, low_part = high_and_low(p)
                        v.tensor_tensor(low_part, mix_slot(p), high_part, ALU.subtract).then_inc(low_dve, 1)

                def norm(which, gain, permuted):
                    link(v.tensor_tensor_reduce(xn[:, D:2 * D], x[:, 1, :], x[:, 1, :], 1.0, 0.0, ALU.mult, ALU.add, ss[:, 1:2]))
                    dve.wait_ge(ss_act, l * 2 + which + 1)
                    rstd_from(ss[:, :], 1.0 / D, 2 * which)
                    newton_step(2 * which).then_inc(rstd_dve, 1)
                    dve.wait_ge(rstd_dve, l * 2 + which + 1)
                    dst, src = xn[:, D:2 * D], x[:, 1, :]
                    if permuted:
                        dst = dst.rearrange("p (c q) -> p c q", c=KC)
                        src = src.rearrange("p (q c) -> p c q", c=KC)
                    v.tensor_scalar(dst, src, rstd[:, 1:2], None, ALU.mult).then_inc(xn_dve, 1)
                    if which == 0:
                        low(*unit_slots(0))
                        for b in range(4):
                            dve.wait_ge(hT_act, l * 6 + b + 1)
                            for c in range(2):
                                m = 2 * b + c
                                ins = v.scalar_tensor_tensor(hT_low[:, m, :], (psA, psB)[b // 2][:, b % 2, c * S:(c + 1) * S],
                                                             gain[:, m:m + 1], hT_high[:, m, :], ALU.mult, ALU.subtract)
                            ins.then_inc(hT_dve, 1)
                        low(*unit_slots(1))
                        return
                    for b, ps in ((1, psA), (3, psB)):
                        dve.wait_ge(hT_ps, l * 8 + which * 4 + b + 1)
                        v.tensor_tensor(hT[:, 2 * b:2 * b + 2, :], ps[:, 1, :].rearrange("p (c s) -> p c s", c=2),
                                        gain[:, 2 * b:2 * b + 2].unsqueeze(2).to_broadcast([P, 2, S]), ALU.mult).then_inc(hT_dve, 1)

                def result(n):
                    dve.wait_ge(mixed, l * N_RESULTS + n + 1)
                    return (psA, psB)[n % 2]

                v.tensor_copy(w_conv[:, :], cols[:, bass.ds(l * (4 * CONV) + DEPTH * KC, 4 * CONV)])
                v.tensor_copy(g_ffn[:, :], g_ffn_all[:, bass.ds(l, 1), :].rearrange("p l c -> p (l c)"))
                v.tensor_copy(r_w[:, :, 0:NG], rg_all[:, bass.ds(l, 1), :, :].rearrange("p l c n -> p (l c) n"))
                v.tensor_copy(r_w[:, :, NG:], re_all[:, bass.ds(l, 1), :, :].rearrange("p l c n -> p (l c) n"))
                v.tensor_copy(r_b[:, 0:NG], rgb_all[:, bass.ds(l, 1), :].rearrange("p l n -> p (l n)"))
                v.tensor_copy(r_b[:, NG:], reb_all[:, bass.ds(l, 1), :].rearrange("p l n -> p (l n)"))
                v.tensor_copy(g_mix[:, :], cols[:, bass.ds(l * KC, KC)]).then_inc(layer_cols, 1)
                dve.wait_ge(layer_cols, l + 1)
                dve.wait_ge(x_landed, 16 * NT)
                norm(0, g_mix, False)

                def rope(view, cos_t, sin_t, heads, half):
                    n = NT * heads * half
                    t4 = [tmp[:, i * n:(i + 1) * n].rearrange("p (t h i) -> p t h i", t=NT, h=heads) for i in range(4)]
                    x1, x2 = view[:, :, :, 0:half], view[:, :, :, half:2 * half]
                    cb = cos_t.unsqueeze(2).to_broadcast([P, NT, heads, half])
                    sb_ = sin_t.unsqueeze(2).to_broadcast([P, NT, heads, half])
                    v.tensor_tensor(t4[0], x1, cb, ALU.mult)
                    v.tensor_tensor(t4[1], x2, sb_, ALU.mult)
                    v.tensor_tensor(t4[2], x1, sb_, ALU.mult)
                    link(v.tensor_tensor(t4[3], x2, cb, ALU.mult))
                    v.tensor_tensor(x1, t4[0], t4[1], ALU.subtract)
                    return v.tensor_tensor(x2, t4[2], t4[3], ALU.add)

                dve.wait_ge(act_out, l * len(on_act) + 1 + on_act.index(G_QI))
                dve.wait_ge(trig_act, 1)
                heads5 = idx[:, :, 0:320].rearrange("p t (h w) -> p t h w", h=IH + 1)
                link(rope(heads5, cos[:, :, 0::2], sin[:, :, 0::2], IH + 1, IROT))
                v.tensor_scalar(wi[:, :, :], idx[:, :, 384:388], IDX_W_SCALE, None, ALU.mult)
                v.tensor_copy(idx[:, :, 320:384], idx[:, :, 256:320]).then_inc(idx_roped, 1)
                low(*unit_slots(2))
                dve.wait_ge(act_out, l * len(on_act) + 1 + on_act.index(G_Q))
                rope(q_tok.rearrange("p t (h w) -> p t h w", h=HEADS), cos[:, :, :], sin[:, :, :], HEADS, ROT).then_inc(q_roped, 1)
                low(*unit_slots(3))
                dve.wait_ge(act_out, l * len(on_act) + 1 + on_act.index(G_K))
                dve.wait_ge(q_roped, l + 1)
                rope(k_tok.rearrange("p t (h w) -> p t h w", h=HEADS), cos[:, :, :], sin[:, :, :], HEADS, ROT).then_inc(k_roped, 1)
                low(*unit_slots(4))

                for b, terms, nk in ((0, p0, P), (1, rel, S)):
                    limit = causal[:, S - nk:S]
                    dve.wait_ge(rel_act, l * 2 + b + 1)
                    for h in range(IH):
                        link(v.scalar_tensor_tensor(score[:, 0:nk], terms[:, h, 0:nk], wi[:, b, h:h + 1],
                                                    limit if h == 0 else score[:, 0:nk], ALU.mult, ALU.add), h == IH - 1)
                    for r in range(TOPK // 8):
                        left = score if r == 0 else work
                        link(v.max(top8[:, :], left[:, 0:nk]), True)
                        link(v.match_replace(work[:, 0:nk], top8[:, :], left[:, 0:nk], TAKEN), r < TOPK // 8 - 1)
                    link(v.tensor_tensor(maskb[:, b, 0:nk], work[:, 0:nk], score[:, 0:nk], ALU.is_equal))
                    link(v.scalar_tensor_tensor(maskb[:, b, 0:nk], maskb[:, b, 0:nk], NEG, limit, ALU.mult, ALU.add))
                    if b == 0:
                        low(*unit_slots(5))

                dve.wait_ge(act_out, l * len(on_act) + 1 + on_act.index(G_VA))
                for t in range(NT):
                    ins = v.bn_stats(stats[:, t, :], vg[:, t, :])
                link(ins, True)
                for t in range(NT):
                    ins = v.bn_aggr(mv[:, t, :], stats[:, t, :])
                link(ins)
                rstd_from(mv[:, :, 1], 1.0, 1)
                low(*unit_slots(6))

                for b, pr, nk in ((0, p0, P), (1, rel, S)):
                    dve.wait_ge(logit_ps, l * 2 + b + 1)
                    if b == 0:
                        src = psD[:, 0, :].rearrange("p (h s) -> p h s", h=HEADS)
                        link(v.scalar_tensor_tensor(pr[:, :, 0:nk], src, LOGIT_SCALE,
                                                    maskb[:, b:b + 1, 0:nk].to_broadcast([P, HEADS, nk]), ALU.mult, ALU.add))
                    else:
                        for r in range(2):
                            src = psC[:, r, :].rearrange("p (h s) -> p h s", h=2)
                            ins = v.scalar_tensor_tensor(pr[:, 2 * r:2 * r + 2, 0:nk], src, LOGIT_SCALE,
                                                         maskb[:, b:b + 1, 0:nk].to_broadcast([P, 2, nk]), ALU.mult, ALU.add)
                        link(ins)
                    link(v.tensor_reduce(mx[:, b, :], pr[:, :, 0:nk], AX.X, ALU.max))
                    v.tensor_scalar(mx[:, b, :], mx[:, b, :], -1.0, None, ALU.mult).then_inc(exp_args, 1)

                low(*unit_slots(7))
                zz = z[:, :, CONV - 1:].rearrange("p (b m) s -> p b m s", b=2)
                v.tensor_copy(zz, result(G_CX)[:, :, :].rearrange("p b (m s) -> p b m s", m=2)).then_inc(dve_out, 1)
                dve.wait_ge(dve_out, l * len(on_dve) + 1 + on_dve.index(G_CX))

                for b, pr, nk in ((0, p0, P), (1, rel, S)):
                    dve.wait_ge(exp_act, l * 2 + b + 1)
                    link(v.reciprocal(rden[:, b, :], den[:, b, :]))
                    v.tensor_tensor(pr[:, :, 0:nk], pr[:, :, 0:nk],
                                    rden[:, b, :].unsqueeze(2).to_broadcast([P, HEADS, nk]), ALU.mult).then_inc(probs, 1)

                low(*unit_slots(8))
                link(newton_step(1))
                for t in range(NT):
                    ins = v.tensor_scalar(vg[:, t, :], vg[:, t, :], mv[:, t, 0:1], rstd[:, t:t + 1], ALU.subtract, ALU.mult)
                ins.then_inc(v_normed, 1)

                ps = result(G_CC)
                v.tensor_tensor(zz, ps[:, :, :].rearrange("p b (m s) -> p b m s", m=2), zz, ALU.mult).then_inc(dve_out, 1)
                dve.wait_ge(dve_out, l * len(on_dve) + 1 + on_dve.index(G_CC))
                low(*unit_slots(9))
                yc = tmp[:, :].rearrange("p (m s) -> p m s", m=4)
                for k in range(CONV):
                    for m in range(4):
                        wk = w_conv[:, k * 4 + m:k * 4 + m + 1]
                        if k == 0:
                            ins = v.tensor_scalar(yc[:, m, :], z[:, m, 0:S], wk, None, ALU.mult)
                        else:
                            ins = v.scalar_tensor_tensor(yc[:, m, :], z[:, m, k:k + S], wk, yc[:, m, :], ALU.mult, ALU.add)
                    link(ins)
                ps = result(G_CB)
                v.tensor_tensor(ycT[:, :, :].rearrange("p (b m) s -> p b (m s)", b=2), ps[:, :, :],
                                tmp[:, :].rearrange("p (b n) -> p b n", b=2), ALU.mult).then_inc(dve_out, 1)
                low(*unit_slots(10))
                dve.wait_ge(ybT_act, l + 1)
                v.tensor_tensor(yb_low.rearrange("p (b h) s -> p b (h s)", b=2), psD[:, :, :],
                                ybT[:, :, :].rearrange("p (b h) s -> p b (h s)", b=2), ALU.subtract).then_inc(branch_low_dve, 1)
                dve.wait_ge(branch_act, l * 2 + 1)
                v.tensor_tensor(branch_low[2][:, :, :], ycT[:, :, :], branch_high[2][:, :, :], ALU.subtract).then_inc(branch_low_dve, 1)
                low(*unit_slots(11))

                dve.wait_ge(vm_ps, l + 1)
                dve.wait_ge(act_out, l * len(on_act) + 1 + on_act.index(G_U))
                uu = uT[:, :, :].rearrange("p (b h) s -> p b (h s)", b=2)
                v.tensor_tensor(uu, uu, psC[:, :, :], ALU.mult).then_inc(yaT_done, 1)
                low(*unit_slots(12))
                dve.wait_ge(branch_act, l * 2 + 2)
                v.tensor_tensor(branch_low[0][:, :, :], uT[:, :, :], ya_high, ALU.subtract).then_inc(branch_low_dve, 1)
                for unit in range(13, 17):
                    low(*unit_slots(unit))

                def merged_part(half):
                    dve.wait_ge(merged_act, l * 2 + half + 1)
                    part = slice(4 * half, 4 * half + 4)
                    v.tensor_tensor(merged_low[:, part, :], merged[:, part, :], merged_high[:, part, :],
                                    ALU.subtract).then_inc(merged_low_dve, 1)

                dve.wait_ge(act_out, (l + 1) * len(on_act))
                for half in range(2):
                    dst = merged[:, 4 * half:4 * half + 4, :].rearrange("p (b h) s -> p b (h s)", b=2)
                    t2 = tmp[:, :].rearrange("p (b n) -> p b n", b=2)
                    for branch in range(3):
                        n = N_IN + 3 * half + branch
                        gate = gates[:, 2 * branch + half].rearrange("p (b h) s -> p b (h s)", b=2)
                        v.tensor_tensor(dst if branch == 0 else t2, result(n)[:, :, :], gate, ALU.mult).then_inc(dve_out, 1)
                        dve.wait_ge(dve_out, l * len(on_dve) + 1 + on_dve.index(n))
                        if branch:
                            ins = v.tensor_tensor(dst, dst, t2, ALU.add)
                        if branch == 1:
                            link(ins)
                        if n == N_IN + 1:
                            low(*unit_slots(17))
                        if n == N_IN + 3:
                            merged_part(0)
                            low(*unit_slots(18))
                    ins.then_inc(merged_done, 1)
                    dve.wait_ge(merged_done, l * 2 + half + 1)
                low(*unit_slots(19))
                merged_part(1)
                for half in range(2):
                    n = N_IN + N_PROJ + half
                    dst = x[:, :, 512 * half:512 * half + 512]
                    v.tensor_tensor(dst, dst, result(n)[:, :, :], ALU.add).then_inc(dve_out, 1)
                dve.wait_ge(dve_out, (l + 1) * len(on_dve))

                norm(1, g_ffn, True)
                dve.wait_ge(route_ps, l + 1)
                lg = psC[:, 0, 0:NT * N_ROUTE].rearrange("p (t n) -> p t n", t=NT)
                v.tensor_tensor(elog[:, :, :, :].rearrange("p t g e -> p t (g e)"), lg[:, :, NG:],
                                r_b[:, NG:].unsqueeze(1).to_broadcast([P, NT, NE]), ALU.add)
                link(v.tensor_tensor(glog[:, :, 0:NG], lg[:, :, 0:NG],
                                     r_b[:, 0:NG].unsqueeze(1).to_broadcast([P, NT, NG]), ALU.add), True)
                for t in range(NT):
                    ins = v.max(gtop[:, t, :], glog[:, t, :])
                link(ins, True)
                for t in range(NT):
                    ins = v.max_index(gtop_i[:, t, :], gtop[:, t, :], glog[:, t, :])
                link(ins)
                v.tensor_tensor(ex[:, :, 0:NG], glog[:, :, 0:NG], gtop[:, :, 0:1].to_broadcast([P, NT, NG]), ALU.subtract)
                link(v.tensor_copy(gidx[:, :], gtop_i[:, :, 0]))
                link(v.tensor_tensor(goh[:, :, :], iota[:, 0:NG].unsqueeze(1).to_broadcast([P, NT, NG]),
                                     gidx[:, :].unsqueeze(2).to_broadcast([P, NT, NG]), ALU.is_equal))
                v.tensor_scalar(gpen[:, :, :], goh[:, :, :], -NEG, NEG, ALU.mult, ALU.add)
                e3 = em[:, :, :, :].rearrange("p t g e -> p (t g) e")
                link(v.tensor_tensor(e3, elog[:, :, :, :].rearrange("p t g e -> p (t g) e"),
                                     goh[:, :, :].rearrange("p t g -> p (t g)").unsqueeze(2).to_broadcast([P, NT * NG, EPG]), ALU.mult))
                link(v.tensor_tensor(e3, e3, gpen[:, :, :].rearrange("p t g -> p (t g)").unsqueeze(2).to_broadcast([P, NT * NG, EPG]),
                                     ALU.add), True)
                for t in range(NT):
                    ins = v.max(etop[:, t, :], em[:, t].rearrange("p g e -> p (g e)"))
                link(ins, True)
                for t in range(NT):
                    ins = v.max_index(etop_i[:, t, :], etop[:, t, :], em[:, t].rearrange("p g e -> p (g e)"))
                link(ins)
                v.tensor_tensor(ex[:, :, NG:NG + 1], etop[:, :, 1:2], etop[:, :, 0:1], ALU.subtract).then_inc(route_args, 1)
                link(v.tensor_copy(eidx[:, :, :], etop_i[:, :, 0:2]))
                for k, oh in ((0, oh0), (1, oh1)):
                    ins = v.tensor_tensor(oh[:, :, :], iota[:, 0:NE].unsqueeze(1).to_broadcast([P, NT, NE]),
                                          eidx[:, :, k:k + 1].to_broadcast([P, NT, NE]), ALU.is_equal)
                link(ins)
                v.tensor_tensor(member[:, :, :], oh0[:, :, :], oh1[:, :, :], ALU.add).then_inc(members, 1)
                dve.wait_ge(route_exp, l + 1)
                link(v.tensor_reduce(gsum[:, :], ex[:, :, 0:NG], AX.X, ALU.add))
                link(v.scalar_tensor_tensor(tw[:, :, 1:2], ex[:, :, NG:NG + 1], 1.0, gsum[:, :].unsqueeze(2), ALU.add, ALU.mult))
                link(v.reciprocal(tw[:, :, 0:1], tw[:, :, 1:2]))
                link(v.tensor_tensor(tw[:, :, 1:2], tw[:, :, 0:1], ex[:, :, NG:NG + 1], ALU.mult))
                v.tensor_tensor(oh0[:, :, :], oh0[:, :, :], tw[:, :, 0:1].to_broadcast([P, NT, NE]), ALU.mult)
                link(v.tensor_tensor(oh1[:, :, :], oh1[:, :, :], tw[:, :, 1:2].to_broadcast([P, NT, NE]), ALU.mult))
                v.tensor_tensor(wt_tab[:, :, 0:NE], oh0[:, :, :], oh1[:, :, :], ALU.add)
                dve.wait_ge(rank_ps, l + 1)
                rk = psD[:, 0, 0:2 * NE].rearrange("p (t e) -> p t e", t=NT)
                link(v.scalar_tensor_tensor(pos_tab[:, :, 0:NE], rk, 1.0, member[:, :, :], ALU.add, ALU.mult))
                v.tensor_scalar(pos_tab[:, :, 0:NE], pos_tab[:, :, 0:NE], -1.0, None, ALU.add)
                nb = S // BLK - 1
                link(v.tensor_tensor(beyond[:, :, :], psD[:, 0, 2 * NE:3 * NE].unsqueeze(2).to_broadcast([P, NE, nb]),
                                     thresholds[:, :].unsqueeze(1).to_broadcast([P, NE, nb]), ALU.is_gt))
                link(v.tensor_reduce(cumA[:, 16:], beyond[:, :, :], AX.X, ALU.add))
                link(v.tensor_reduce(total[:, :], cumA[:, 16:], AX.X, ALU.add))
                link(v.tensor_scalar(nquad[:, :], bidx[:, 0:OVER_BLOCKS:QB], total[:, 0:1], None, ALU.is_lt))
                link(v.tensor_reduce(total[:, :], nquad[:, :], AX.X, ALU.add))
                link(v.scalar_tensor_tensor(quads_f[:, :], total[:, :], float(MAIN_QUADS), quads_f[:, :], ALU.add, ALU.add))
                v.tensor_copy(quads_i[:, bass.ds(l + 1, 1)], quads_f[:, :]).then_inc(quads_known, 1)

                def choose(i, g):
                    blk = i * QB
                    iota_b = iota[:, :].unsqueeze(1).unsqueeze(1).to_broadcast([P, NT, QB, BLK])
                    v.tensor_tensor(sel, pos_tab[:, :, bass.ds(blk, QB)].unsqueeze(3).to_broadcast([P, NT, QB, BLK]),
                                    iota_b, ALU.is_equal).then_inc(quad_link, 1)
                    dve.wait_ge(quad_link, g + l + 1)
                    v.tensor_tensor(selw, sel, wt_tab[:, :, bass.ds(blk, QB)].unsqueeze(3).to_broadcast([P, NT, QB, BLK]),
                                    ALU.mult).then_inc(sel_done, 1)

                def gathered(g):
                    dve.wait_ge(gather_ps, g + l + 1)
                    for b in range(2):
                        ins = v.tensor_tensor(xT[:, 4 * b:4 * b + 4, :], psA[:, b, :].rearrange("p (c n) -> p c n", c=4),
                                              g_ffn[:, 4 * b:4 * b + 4].unsqueeze(2).to_broadcast([P, 4, P]), ALU.mult)
                    ins.then_inc(xT_done, 1)

                def add_rows(g):
                    for t in range(NT):
                        dve.wait_ge(scatter_ps[t], g + 1)
                        v.tensor_tensor(x[:, t, :].rearrange("p (b n) -> p b n", b=2), x[:, t, :].rearrange("p (b n) -> p b n", b=2),
                                        psA[:, :, :], ALU.add).then_inc(x_added, 1)

                def choose_next(i, g):
                    dve.wait_ge(selT_ps, g + 1)
                    choose(i + 1, g + 1)

                def pair_rest(g):
                    dve.wait_ge(quad_freed, g * STAGES + STAGES + 4)
                    dve.wait_ge(silu_act, g + 1)
                    v.tensor_tensor(hid, silu, psB[:, 1, :], ALU.mult).then_inc(hid_done, 1)
                    gathered(g + 1)
                    dve.wait_ge(quad_freed, g * STAGES + 2 * STAGES)
                    v.tensor_copy(y[:, 1, :], psC[:, 1, :]).then_inc(y_dve, 1)

                def overflow_tables():
                    src, dst = cumA, cumB
                    for s in (1, 2, 4, 8, 16):
                        link(v.tensor_tensor(dst[:, 16:], src[:, 16:], src[:, 16 - s:16 + NE - s], ALU.add))
                        src, dst = dst, src
                    cum = src[:, 16:].unsqueeze(1).to_broadcast([P, TAB_BLOCKS, NE])
                    link(v.tensor_tensor(over1, cum, bidx[:, :].unsqueeze(2).to_broadcast([P, TAB_BLOCKS, NE]), ALU.is_le))
                    v.tensor_reduce(over_e[:, :], over1, AX.X, ALU.add)
                    link(v.tensor_tensor(over2, over1, cum, ALU.mult))
                    link(v.tensor_reduce(over_prev[:, :], over2, AX.X, ALU.max))
                    link(v.tensor_tensor(over_prev[:, :], bidx[:, :], over_prev[:, :], ALU.subtract))
                    v.tensor_scalar(over_prev[:, :], over_prev[:, :], 1.0, float(BLK), ALU.add, ALU.mult)
                    v.tensor_scalar(over_i[:, :], over_e[:, :], float(NE - 1), None, ALU.min).then_inc(over_known, 1)
                    link(v.tensor_tensor(over1, iota[:, 0:NE].unsqueeze(1).to_broadcast([P, TAB_BLOCKS, NE]),
                                         over_e[:, :].unsqueeze(2).to_broadcast([P, TAB_BLOCKS, NE]), ALU.is_equal))
                    for t in range(NT):
                        link(v.tensor_tensor(over2, over1, pos_tab[:, t:t + 1, 0:NE].to_broadcast([P, TAB_BLOCKS, NE]), ALU.mult))
                        link(v.tensor_reduce(over_r[:, :], over2, AX.X, ALU.add))
                        v.tensor_tensor(pos_tab[:, t, NE:], over_r[:, :], over_prev[:, :], ALU.subtract)
                        link(v.tensor_tensor(over2, over1, wt_tab[:, t:t + 1, 0:NE].to_broadcast([P, TAB_BLOCKS, NE]), ALU.mult))
                        link(v.tensor_reduce(wt_tab[:, t, NE:], over2, AX.X, ALU.add))

                dve.wait_ge(quads_known, l + 2)
                alone(dve)
                start = dve.value_load(quads_i[0:1, bass.ds(l, 1)], min_val=0, max_val=DEPTH * MAX_QUADS)
                end = dve.value_load(quads_i[0:1, bass.ds(l + 1, 1)], min_val=MAIN_QUADS, max_val=DEPTH * MAX_QUADS)
                choose(0, start)
                gathered(start)
                choose_next(0, start)
                overflow_tables()
                pair_rest(start)
                with dve.Fori(0, nc.s_assert_within(end - start - 1, MAIN_QUADS - 1, MAX_QUADS - 1)) as i:
                    add_rows(start + i)
                    choose_next(i + 1, start + i + 1)
                    pair_rest(start + i + 1)
                add_rows(end - 1)
                dve.wait_ge(x_added, end * 2 + 1)
                assert linked[0] == DVE_MIX, f"DVE_MIX = {linked[0]}"

            link_n = [0]

            def last(ins):
                link_n[0] += 1
                ins.then_inc(final_link, 1)
                dve.wait_ge(final_link, link_n[0])

            last(v.tensor_tensor_reduce(xn[:, D:2 * D], x[:, 1, :], x[:, 1, :], 1.0, 0.0, ALU.mult, ALU.add, ss[:, 1:2]))
            dve.wait_ge(ss_act, 2 * DEPTH + 1)
            last(v.tensor_scalar(var[:, :], ss[:, :], 1.0 / D, EPS, ALU.mult, ALU.add))
            v.reciprocal(inv[:, :], var[:, :]).then_inc(inv_dve, 1)
            dve.wait_ge(root, 3 * DEPTH + 1)
            last(v.tensor_tensor(newton[:, :], rstd[:, :], rstd[:, :], ALU.mult))
            last(v.tensor_tensor(newton[:, :], newton[:, :], var[:, :], ALU.mult))
            last(v.tensor_scalar(newton[:, :], newton[:, :], -0.5, 1.5, ALU.mult, ALU.add))
            last(v.tensor_tensor(rstd[:, :], rstd[:, :], newton[:, :], ALU.mult))
            dve.wait_ge(gfin_landed, 16)
            for t in range(NT):
                v.scalar_tensor_tensor(xn[:, t * D:(t + 1) * D], x[:, t, :], rstd[:, t:t + 1], gfin[:, :],
                                       ALU.mult, ALU.mult).then_inc(final_done, 1)

        def tensor_program(pe):
            te = nc.tensor
            pe.wait_ge(consts, 3)
            pe.wait_ge(small_landed, 16 * N_SMALL)
            n_rows = rows.shape[0]
            te.transpose(psD[:, 1, 0:n_rows], rows[:, :], ident[0:n_rows, 0:n_rows]).then_inc(cols_ps, 1)
            with pe.Fori(0, DEPTH) as l:
                pe.wait_ge(quads_known, l + 1)
                alone(pe)
                done = pe.value_load(quads_i[0:1, bass.ds(l, 1)], min_val=0, max_val=DEPTH * MAX_QUADS)

                def split(p):
                    pe.wait_ge(low_dve, l * MIX_SLOTS + p - PAD + 1)
                    return [w.rearrange("p (c n) -> p c n", c=4) for w in high_and_low(p)]

                TERMS = ((0, 0), (0, 1), (1, 0))

                def product(o, xs, ws, weights_stationary, start, stop):
                    for i, (a, b) in enumerate(TERMS):
                        first, second = (ws[b], xs[a]) if weights_stationary else (xs[a], ws[b])
                        ins = te.matmul(o, first, second, start=start and i == 0, stop=stop and i == len(TERMS) - 1)
                    return ins

                def free_result(n):
                    if n < 2:
                        return
                    if n - 2 in on_act:
                        pe.wait_ge(act_out, l * len(on_act) + 1 + on_act.index(n - 2))
                    else:
                        pe.wait_ge(dve_out, l * len(on_dve) + 1 + on_dve.index(n - 2))

                def norm_transposes(which):
                    pe.wait_ge(xn_act, l * 2 + which + 1)
                    pe.wait_ge(xn_dve, l * 2 + which + 1)
                    for b in range(4):
                        ps = (psA, psB)[b // 2]
                        for c in range(2):
                            for t in range(NT):
                                o = t * D + (2 * b + c) * P
                                ins = te.transpose(ps[:, b % 2, c * S + t * P:c * S + t * P + P], xn[:, o:o + P], ident[:, :])
                        ins.then_inc(hT_ps, 1)
                    pe.wait_ge(hT_act, l * 6 + 4 + which * 2)
                    pe.wait_ge(hT_dve, l * 6 + 4 + which * 2)

                def group(g):
                    token_major = g in (G_QI, G_Q, G_K, G_V, G_VA)
                    n = N_IDX if g == G_QI else WB
                    ps = (psA, psB)[g % 2]
                    w = [split(p) for p in unit_slots(g)]
                    free_result(g)
                    for m in range(NT if token_major else 4):
                        for c in range(KC):
                            ends = c == 0, c == KC - 1
                            if token_major:
                                ins = product(ps[:, m, 0:n], [h[:, c, m * P:(m + 1) * P] for h in (hT_high, hT_low)],
                                              [wp[:, c % 4, :] for wp in w[c // 4]], False, *ends)
                            else:
                                ins = product(ps[:, m // 2, (m % 2) * S:(m % 2 + 1) * S], [h[:, c, :] for h in (hT_high, hT_low)],
                                              [wp[:, c % 4, m * P:(m + 1) * P] for wp in w[c // 4]], True, *ends)
                    ins.then_inc(mixed, 1)

                def index_transposes():
                    pe.wait_ge(idx_roped, l + 1)
                    for a in range(3):
                        for t in range(NT):
                            o = psC[:, 0, a * S + t * P:a * S + t * P + P] if a < 2 else psC[:, 1, t * P:t * P + P]
                            ins = te.transpose(o, idx[:, t, a * P:(a + 1) * P], ident[:, :])
                    ins.then_inc(idxT_ps, 1)

                def index_scores():
                    pe.wait_ge(idxT_act, l + 1)
                    for b, ps, nk in ((0, psD, P), (1, psC, S)):
                        for h in range(IH):
                            r = h % 2
                            a = h // 2
                            ins = te.matmul(ps[:, r, a * nk:(a + 1) * nk], qiT[IDIM * r:IDIM * (r + 1), a, b * P:(b + 1) * P],
                                            kiT[IDIM * r:IDIM * (r + 1), 0:nk], start=True, stop=True)
                        ins.then_inc(score_ps, 1)

                def head_transposes(src, ps, ready, freed, done_sem):
                    pe.wait_ge(ready, l + 1)
                    freed()
                    for h in range(HEADS):
                        for t in range(NT):
                            o = (h % 2) * S + t * P
                            ins = te.transpose(ps[:, h // 2, o:o + P], src[:, t, h * HD:(h + 1) * HD], ident[:, :])
                    ins.then_inc(done_sem, 1)

                def logits():
                    pe.wait_ge(qT_act, l + 1)
                    pe.wait_ge(kT_act, l + 1)
                    for h in range(HEADS):
                        ins = te.matmul(psD[:, 0, h * P:(h + 1) * P], qT[:, h, 0:P], kT[:, h, 0:P], start=True, stop=True)
                    ins.then_inc(logit_ps, 1)
                    for h in range(HEADS):
                        ins = te.matmul(psC[:, h // 2, (h % 2) * S:(h % 2 + 1) * S], qT[:, h, P:S], kT[:, h, :], start=True, stop=True)
                    ins.then_inc(logit_ps, 1)

                def prob_transposes():
                    pe.wait_ge(probs, l * 2 + 1)
                    for h in range(HEADS):
                        ins = te.transpose(psD[:, 1, h * P:(h + 1) * P], p0[:, h, :], ident[:, :])
                    ins.then_inc(pT_ps, 1)
                    pe.wait_ge(probs, l * 2 + 2)
                    for k in range(2):
                        for h in range(HEADS):
                            ins = te.transpose(psC[:, k, h * P:(h + 1) * P], rel[:, h, k * P:(k + 1) * P], ident[:, :])
                    ins.then_inc(pT_ps, 1)

                def attend():
                    pe.wait_ge(pT_act, l + 1)
                    for h in range(HEADS):
                        o = (h % 2) * S
                        te.matmul(psD[:, h // 2, o:o + P], v_tok[:, 0, h * HD:(h + 1) * HD], pT[:, 0, h, :], start=True, stop=True)
                        for k in range(2):
                            ins = te.matmul(psD[:, h // 2, o + P:o + S], v_tok[:, k, h * HD:(h + 1) * HD], pT[:, 1 + k, h, :],
                                            start=k == 0, stop=k == 1)
                    ins.then_inc(ybT_ps, 1)

                def spatial_transposes():
                    pe.wait_ge(ws_landed, l * 32 + 32)
                    for h in range(HEADS):
                        ins = te.transpose(psC[:, 0, h * P:(h + 1) * P], ws_raw[:, h, :], ident[:, :])
                    ins.then_inc(wsT_ps, 1)

                def spatial():
                    pe.wait_ge(tri_done, l + 1)
                    pe.wait_ge(v_normed, l + 1)
                    for h in range(HEADS):
                        for t in range(NT):
                            o = psC[:, h // 2, (h % 2) * S + t * P:(h % 2) * S + (t + 1) * P]
                            te.matmul(o, vg[:, t, h * HD:(h + 1) * HD], wsT[:, h, :], start=True, stop=False)
                            ins = te.matmul(o, ones[0:1, :], bs_row[0:1, h * P:(h + 1) * P], start=False, stop=True)
                    ins.then_inc(vm_ps, 1)

                norm_transposes(0)
                group(G_QI)
                group(G_Q)
                index_transposes()
                group(G_K)
                index_scores()
                group(G_V)
                head_transposes(q_tok, psD, q_roped, lambda: pe.wait_ge(rel_act, l * 2 + 1), qT_ps)
                group(G_VA)
                head_transposes(k_tok, psC, k_roped, lambda: pe.wait_ge(rel_act, l * 2 + 2), kT_ps)
                group(G_U)
                logits()
                group(G_CX)
                group(G_CC)
                prob_transposes()
                group(G_CB)
                attend()
                spatial_transposes()
                group(G_GATE0)
                group(G_GATE0 + 1)
                spatial()
                for n in range(2, 6):
                    group(G_GATE0 + n)

                for k in range(N_PROJ):
                    n = N_IN + k
                    p = PAD + 2 * N_IN + k
                    branch = k % 3
                    if k == 0:
                        pe.wait_ge(branch_low_dve, l * 3 + 3)
                    w = split(p)
                    free_result(n)
                    for m in range(4):
                        for c in range(4):
                            ins = product((psA, psB)[n % 2][:, m // 2, (m % 2) * S:(m % 2 + 1) * S],
                                          [part[:, c, :] for part in (branch_high[branch], branch_low[branch])],
                                          [wp[:, c, m * P:(m + 1) * P] for wp in w], True, c == 0, c == 3)
                    ins.then_inc(mixed, 1)
                for part in range(2):
                    for half in range(2):
                        n = N_IN + N_PROJ + half
                        w = split(P_OUT[part, half])
                        if part == 0:
                            free_result(n)
                        if half == 0:
                            pe.wait_ge(merged_low_dve, l * 2 + part + 1)
                        for t in range(NT):
                            for c in range(4):
                                m = 4 * part + c
                                ins = product((psA, psB)[n % 2][:, t, :], [h[:, m, t * P:(t + 1) * P] for h in (merged_high, merged_low)],
                                              [wp[:, c, :] for wp in w], False, m == 0, m == KC - 1)
                        if part == 1:
                            ins.then_inc(mixed, 1)

                norm_transposes(1)
                for t in range(NT):
                    for c in range(KC):
                        ins = te.matmul(psC[:, 0, t * N_ROUTE:(t + 1) * N_ROUTE], hT[:, c, t * P:(t + 1) * P], r_w[:, c, :],
                                        start=c == 0, stop=c == KC - 1)
                ins.then_inc(route_ps, 1)
                pe.wait_ge(members, l + 1)
                te.matmul(psD[:, 0, 0:NE], before[:, :], member[:, 0, :], start=True, stop=True)
                te.matmul(psD[:, 0, NE:2 * NE], ones[:, :], member[:, 0, :], start=True, stop=False)
                te.matmul(psD[:, 0, NE:2 * NE], before[:, :], member[:, 1, :], start=False, stop=True)
                te.matmul(psD[:, 0, 2 * NE:3 * NE], ones[:, :], member[:, 0, :], start=True, stop=False)
                te.matmul(psD[:, 0, 2 * NE:3 * NE], ones[:, :], member[:, 1, :], start=False, stop=True).then_inc(rank_ps, 1)

                pe.wait_ge(quads_known, l + 2)
                alone(pe)
                end = pe.value_load(quads_i[0:1, bass.ds(l + 1, 1)], min_val=MAIN_QUADS, max_val=DEPTH * MAX_QUADS)

                def expert_arrived(g, p):
                    s = p % SLOTS
                    pe.wait_ge(landed[s], l * (16 * MIX_USES[s]) + g * 16 + 16 * (MIX_USES[s] + 1))

                def gather(b):
                    for c in range(4 * b, 4 * b + 4):
                        for t in range(NT):
                            o = t * D + c * P
                            ins = te.matmul(psA[:, b, (c % 4) * P:(c % 4 + 1) * P], xn[:, o:o + P],
                                            sel[:, t].rearrange("p j n -> p (j n)"), start=t == 0, stop=t == NT - 1)
                    return ins

                def gate_up(g, k):
                    half, o = k // 2, k % 2
                    for j in range(QB):
                        expert_arrived(g, k * QB + j)
                    for c in range(4):
                        for j in range(QB):
                            w = slot(k * QB + j, SLOT).rearrange("p (c n) -> p c n", c=4)
                            ins = te.matmul(psB[j * BLK:(j + 1) * BLK, o, :], xT[:, 4 * half + c, j * BLK:(j + 1) * BLK], w[:, c, :],
                                            start=half == 0 and c == 0, stop=half == 1 and c == 3)
                    ins.then_inc(quad_freed, 1)

                def down(g, k):
                    for j in range(QB):
                        expert_arrived(g, (4 + k) * QB + j)
                    for c in range(2):
                        for n in range(2):
                            for j in range(QB):
                                w = slot((4 + k) * QB + j, SLOT).rearrange("p (c n) -> p c n", c=2)
                                ins = te.matmul(psC[j * BLK:(j + 1) * BLK, n, :], hidT[:, 2 * k + c, j * BLK:(j + 1) * BLK],
                                                w[:, c, n * 512:(n + 1) * 512], start=k == 0 and c == 0, stop=k == 1 and c == 1)
                    ins.then_inc(quad_freed, 1)

                def scatter(g, t):
                    if t == 0:
                        pe.wait_ge(selT_act, g + 1)
                        pe.wait_ge(y_act, g + 1)
                        pe.wait_ge(y_dve, g + 1)
                    else:
                        pe.wait_ge(x_added, g * 2 + 2)
                    for n in range(2):
                        ins = te.matmul(psA[:, n, :], selwT[:, t, :], y[:, n, :], start=True, stop=True)
                    ins.then_inc(scatter_ps[t], 1)

                def pair(g, first):
                    pe.wait_ge(xT_done, g + l + 1)
                    gate_up(g, 0)
                    if not first:
                        scatter(g - 1, 0)
                    gate_up(g, 1)
                    if not first:
                        scatter(g - 1, 1)
                    for t in range(NT):
                        ins = te.transpose(psD[:, 1, t * P:(t + 1) * P], selw[:, t].rearrange("p j n -> p (j n)"), ident[:, :])
                    ins.then_inc(selT_ps, 1)
                    gate_up(g, 2)
                    gate_up(g, 3)
                    pe.wait_ge(sel_done, g + l + 2)
                    pe.wait_ge(x_added, g * 2 + 1)
                    gather(0)
                    pe.wait_ge(hid_done, g + 1)
                    for c in range(FC):
                        ins = te.transpose(psD[:, 0, c * P:(c + 1) * P], hid[:, c::FC], ident[:, :])
                    ins.then_inc(hidT_ps, 1)
                    gather(1).then_inc(gather_ps, 1)
                    pe.wait_ge(hidT_act, g + 1)
                    for k in range(2):
                        down(g, k)

                pe.wait_ge(sel_done, done + l + 1)
                gather(0)
                gather(1).then_inc(gather_ps, 1)
                pair(done, True)
                with pe.Fori(done + 1, end) as g:
                    pair(g, False)
                for t in range(NT):
                    scatter(end - 1, t)

        TRIG_READY = 11
        final_link = sem("final_link")

        @block.sync
        def _(sp):
            sync_program(sp)

        @block.gpsimd
        def _(pool):
            pool_program(pool)

        @block.scalar
        def _(act):
            scalar_program(act)

        @block.vector
        def _(dve):
            vector_program(dve)

        @block.tensor
        def _(pe):
            tensor_program(pe)


_INS = ['x', 'positions', 'norm_mix_g', 'norm_ffn_g', 'norm_final_g', 'w_in', 'gmlp_ws', 'gmlp_b', 'conv_w',
        'w_proj_a', 'w_proj_b', 'w_proj_c', 'w_out', 'router_group_w', 'router_group_b',
        'router_expert_w', 'router_expert_b', 'expert_w_gate', 'expert_w_up', 'expert_w_down']


def kernel(**inputs):
    import concourse.bacc as _bacc
    from concourse.bass_utils import run_bass_kernel_spmd as _run

    nc = _bacc.Bacc("TRN2", target_bir_lowering=False, num_devices=1)
    arrays, args = {}, []
    for name in _INS:
        a = np.ascontiguousarray(inputs[name])
        arrays[f"in_{name}_dram"] = a
        args.append(nc.dram_tensor(f"in_{name}_dram", a.shape, mybir.dt.from_np(a.dtype), kind="ExternalInput").ap())
    shape = tuple(inputs['x'].shape)
    args.append(nc.dram_tensor("out_0_dram", shape, F32, kind="ExternalOutput").ap())
    build_trunk(nc, *args)
    r = _run(nc, [arrays], core_ids=[0])
    return r.results[0]["out_0_dram"]
```

```python
from contextlib import ExitStack

import numpy as np

import concourse.bass as bass
from concourse import mybir

P = 128
ALU = mybir.AluOpType
ACT = mybir.ActivationFunctionType
AX = mybir.AxisListType
F32 = mybir.dt.float32
F32R = mybir.dt.float32r
I32 = mybir.dt.int32
U32 = mybir.dt.uint32

ROPE_THETA = 500000.0
EPS = 1e-6
NEG = -1e30
TAKEN = -3e38
TWO_PI = 2.0 * np.pi
TWO_PI_HI = 6.28125
TWO_PI_MID = float(np.float32((TWO_PI - TWO_PI_HI) * 2**20 // 1 / 2**20))
TWO_PI_LO = TWO_PI - TWO_PI_HI - TWO_PI_MID
ROUND_MAGIC = 1.5 * 2.0**23


def build_trunk(nc, x_in, positions, norm_mix_g, norm_ffn_g, norm_final_g, w_in, gmlp_ws, gmlp_b, conv_w,
                w_proj_a, w_proj_b, w_proj_c, w_out, router_group_w, router_group_b,
                router_expert_w, router_expert_b, expert_w_gate, expert_w_up, expert_w_down, out):
    _, S, D = x_in.shape
    DEPTH, _, D_IN = w_in.shape
    NT = S // P
    KC = D // P
    HEADS, HD = 4, P
    WB = HEADS * HD
    IH, IDIM = 4, 64
    ROT = HD // 4 // 2
    IROT = IDIM // 4 // 2
    TOPK = min(256, S // 4)
    CONV = conv_w.shape[1]
    NG = router_group_w.shape[2]
    NE = router_expert_w.shape[2]
    EPG = NE // NG
    FF = expert_w_gate.shape[3]
    FC = FF // P
    BLK = 64
    QB = P // BLK
    MAIN_PAIRS = NE // QB
    OVER_BLOCKS = (2 * S) // BLK
    TAB_BLOCKS = OVER_BLOCKS + QB
    MAX_PAIRS = MAIN_PAIRS + OVER_BLOCKS // QB
    assert (S, D, NT, KC, FC) == (256, 1024, 2, 8, 4) and TOPK % 8 == 0 and TOPK <= P
    LOGIT_SCALE = float(HD) ** -0.5
    IDX_SCALE = float(IDIM) ** -0.5
    IDX_W_SCALE = float(IH) ** -0.5
    N_ROUTE = NG + NE

    C_U, C_VA = 0, WB
    C_Q, C_K, C_V = 2 * WB, 3 * WB, 4 * WB
    C_QI = 5 * WB
    N_IDX = IH * IDIM + IDIM + IH
    C_CB = C_QI + N_IDX
    C_CC, C_CX = C_CB + WB, C_CB + 2 * WB
    C_GATE = C_CB + 3 * WB
    assert C_GATE + 3 * D == D_IN

    SLOTS = 12
    SLOT = 2048
    GROUPS = [C_QI, C_Q, C_K, C_V, C_VA, C_U, C_CX, C_CC, C_CB] + [C_GATE + WB * i for i in range(6)]
    G_QI, G_Q, G_K, G_V, G_VA, G_U, G_CX, G_CC, G_CB, G_GATE0 = range(10)
    N_IN = len(GROUPS)
    N_PROJ = 6
    MIX_SLOTS = 2 * N_IN + N_PROJ + 4
    LOW_X = 0
    RING0, MIX_RING = 1, 7
    HIGH0, HIGHS = RING0 + MIX_RING, 4
    assert HIGH0 + HIGHS == SLOTS
    MIX_SPAN = -(-MIX_SLOTS // MIX_RING) * MIX_RING
    PAD = MIX_SPAN - MIX_SLOTS
    PAIR_SLOTS = 6 * QB
    STAGES = 6
    assert PAIR_SLOTS == SLOTS
    N_RESULTS = N_IN + N_PROJ + 2

    def mix_index(p):
        return RING0 + p % MIX_RING

    MIX_USES = [sum(1 for p in range(PAD, MIX_SPAN) if mix_index(p) == s) for s in range(SLOTS)]
    P_OUT = {(part, half): MIX_SPAN - 4 + 2 * part + half for part in range(2) for half in range(2)}

    def result_of(p):
        i = p - PAD
        if i < 2 * N_IN:
            return i // 2 + 1
        i -= 2 * N_IN
        return N_IN + 1 + (i if i < N_PROJ else N_PROJ + (i - N_PROJ) % 2)

    def mixing_reader(s):
        if s == LOW_X:
            return N_IN
        return max(result_of(p) for p in range(PAD, MIX_SPAN) if s in (mix_index(p), HIGH0 + p % HIGHS))

    def words_of(p):
        return 4 * N_IDX if (p - PAD) // 2 == G_QI else SLOT

    DVE_MIX = 116
    TRIG_READY = 11

    with ExitStack() as ctx:
        place = {}

        def sb(name, shape, dt=F32):
            place[name] = -(-nc.sbuf_base // 32) * 32, shape
            return ctx.enter_context(nc.sbuf_tensor(name, shape, dt))

        def rounded(name):
            offset, shape = place[name]
            return nc.alloc_sbuf_tensor_at(name + "_parts", shape, F32R, offset=offset)

        def psum(name):
            return ctx.enter_context(nc.psum_tensor(name, [P, 2, 512], F32))

        def sem(name):
            return ctx.enter_context(nc.semaphore(name))

        psA, psB, psC, psD = psum("psA"), psum("psB"), psum("psC"), psum("psD")

        ring = sb("ring", [P, SLOTS, SLOT])
        x = sb("x", [P, NT, D])
        xn = sb("xn", [P, NT * D])
        hT = sb("hT", [P, KC, S])
        share1 = sb("share1", [P, 2048])
        gates = sb("gates", [P, 6, 4, S])
        idx = sb("idx", [P, NT, 3 * P + IH])
        qiT = sb("qiT", [P, 2, S])
        kiT = sb("kiT", [P, S])
        rel = sb("rel", [P, HEADS, S])
        p0 = sb("p0", [P, HEADS, P])
        score = sb("score", [P, S])
        work = sb("work", [P, S])
        maskb = sb("maskb", [P, NT, S])
        ybT = sb("ybT", [P, HEADS, S], F32R)        
        vg = sb("vg", [P, NT, WB])
        uT = sb("uT", [P, HEADS, S])
        wsT = sb("wsT", [P, HEADS, P])
        bs_row = sb("bs_row", [1, WB])
        z = sb("z", [P, 4, S + CONV - 1])
        ycT = sb("ycT", [P, 4, S])
        tmp = sb("tmp", [P, 1024])

        q_tok = share1[:, 0:1024].rearrange("p (t n) -> p t n", t=NT)
        k_tok = share1[:, 1024:2048].rearrange("p (t n) -> p t n", t=NT)
        merged = share1[:, :].rearrange("p (c s) -> p c s", c=KC)
        qT = xn[:, 0:1024].rearrange("p (h s) -> p h s", h=HEADS)
        kT = xn[:, 1024:2048].rearrange("p (h s) -> p h s", h=HEADS)
        v_tok = gates[:, 5].rearrange("p m s -> p (m s)").rearrange("p (t n) -> p t n", t=NT)
        pT = gates[:, 3:5].rearrange("p g m s -> p (g m s)")[:, 0:3 * WB].rearrange(
            "p (k h q) -> p k h q", k=3, h=HEADS)
        ws_raw = gates[:, 2].rearrange("p m s -> p (m s)")[:, 0:WB].rearrange("p (h s) -> p h s", h=HEADS)
        ring_parts = rounded("ring")
        hT_low = ring_parts[:, LOW_X, :].rearrange("p (c s) -> p c s", c=KC)
        hT_high = rounded("hT")
        merged_high, merged_low = hT_high, rounded("share1")[:, :].rearrange("p (c s) -> p c s", c=KC)
        xn_parts = rounded("xn")
        ya_high, yb_low = [xn_parts[:, i * 1024:(i + 1) * 1024].rearrange("p (c s) -> p c s", c=4) for i in range(2)]
        branch_high = (ya_high, ybT, rounded("rel"))
        branch_low = (rounded("uT"), yb_low, rounded("ycT"))
        xT = share1[:, 0:1024].rearrange("p (c n) -> p c n", c=KC)
        hidT = share1[:, 1024:1536].rearrange("p (c n) -> p c n", c=FC)
        hid = share1[:, 1536:2048]
        y = gates[:, 0].rearrange("p m s -> p (m s)").rearrange("p (n w) -> p n w", n=2)
        silu = gates[:, 1].rearrange("p m s -> p (m s)")[:, 0:512]
        selwT = gates[:, 1].rearrange("p m s -> p (m s)")[:, 512:768].rearrange("p (t n) -> p t n", t=NT)
        sel = gates[:, 2].rearrange("p m s -> p (m s)")[:, 0:256].rearrange("p (t j n) -> p t j n", t=NT, j=QB)
        selw = gates[:, 2].rearrange("p m s -> p (m s)")[:, 256:512].rearrange("p (t j n) -> p t j n", t=NT, j=QB)
        over1 = rel[:, 0:2].rearrange("p h s -> p (h s)")[:, 0:TAB_BLOCKS * NE].rearrange("p (b e) -> p b e", e=NE)
        over2 = rel[:, 2:4].rearrange("p h s -> p (h s)")[:, 0:TAB_BLOCKS * NE].rearrange("p (b e) -> p b e", e=NE)
        gfin = tmp

        ident = sb("ident", [P, P])
        before = sb("before", [P, P])
        ones = sb("ones", [P, P])
        before_r = sb("before_r", [P, P], F32R)
        ones_r = sb("ones_r", [P, P], F32R)
        causal = sb("causal", [P, S])
        iota = sb("iota", [P, NE])
        slots1 = sb("slots1", [P, BLK])
        thresholds = sb("thresholds", [P, S // BLK - 1])
        rows = sb("rows", [DEPTH * (KC + CONV * 4), P])
        cols = sb("cols", [P, DEPTH * (KC + CONV * 4)])
        g_mix = sb("g_mix", [P, KC])
        w_conv = sb("w_conv", [P, CONV * 4])
        g_ffn_all = sb("g_ffn_all", [P, DEPTH, KC])
        g_ffn = sb("g_ffn", [P, KC])
        rg_all = sb("rg_all", [P, DEPTH, KC, NG])
        re_all = sb("re_all", [P, DEPTH, KC, NE])
        rgb_all = sb("rgb_all", [P, DEPTH, NG])
        reb_all = sb("reb_all", [P, DEPTH, NE])
        r_w = sb("r_w", [P, KC, N_ROUTE])
        r_b = sb("r_b", [P, N_ROUTE])
        pos_i = sb("pos_i", [P, NT], I32)
        pos_f = sb("pos_f", [P, NT])
        inv_freq = sb("inv_freq", [P, ROT])
        ang = sb("ang", [P, 3, NT, ROT])
        cos = sb("cos", [P, NT, ROT])
        sin = sb("sin", [P, NT, ROT])

        ss = sb("ss", [P, NT])
        var = sb("var", [P, NT])
        inv = sb("inv", [P, NT])
        rstd = sb("rstd", [P, NT])
        newton = sb("newton", [P, NT])
        stats = sb("stats", [P, NT, 6])
        mv = sb("mv", [P, NT, 2])
        wi = sb("wi", [P, NT, IH])
        top8 = sb("top8", [P, 8])
        mx = sb("mx", [P, NT, HEADS])
        den = sb("den", [P, NT, HEADS])
        rden = sb("rden", [P, NT, HEADS])

        glog = sb("glog", [P, NT, 8])
        gtop = sb("gtop", [P, NT, 8])
        gtop_i = sb("gtop_i", [P, NT, 8], U32)
        gidx = sb("gidx", [P, NT])
        gpen = sb("gpen", [P, NT, NG])
        etop = sb("etop", [P, NT, 8])
        etop_i = sb("etop_i", [P, NT, 8], U32)
        eidx = sb("eidx", [P, NT, 2])
        ex = sb("ex", [P, NT, NG + 1])
        tw = sb("tw", [P, NT, 2])
        gsum = sb("gsum", [P, NT])
        NBL = NE + TAB_BLOCKS
        routing = ycT[:, :, :].rearrange("p m s -> p (m s)")
        taken = [0]

        def part(n):
            taken[0] += n
            return routing[:, taken[0] - n:taken[0]]

        elog = part(NT * NE).rearrange("p (t g e) -> p t g e", t=NT, g=NG)
        em = part(NT * NE).rearrange("p (t g e) -> p t g e", t=NT, g=NG)
        oh0 = part(NT * NE).rearrange("p (t e) -> p t e", t=NT)
        oh1 = part(NT * NE).rearrange("p (t e) -> p t e", t=NT)
        part(NT * NE)
        member = branch_low[2][:, :, :].rearrange("p m s -> p (m s)")[:, taken[0] - NT * NE:taken[0]].rearrange("p (t e) -> p t e", t=NT)
        beyond = part(NE * (S // BLK - 1)).rearrange("p (e k) -> p e k", e=NE)
        pos_tab = part(NT * NBL).rearrange("p (t b) -> p t b", t=NT)
        wt_tab = part(NT * NBL).rearrange("p (t b) -> p t b", t=NT)
        cumA = sb("cumA", [P, 16 + NE])
        cumB = sb("cumB", [P, 16 + NE])
        total = sb("total", [P, 1])
        spare = sb("spare", [P, 1])
        credit = sb("credit", [P, STAGES])
        npair = sb("npair", [P, OVER_BLOCKS // QB])
        pairs_f = sb("pairs_f", [P, 1])
        pairs_i = sb("pairs_i", [P, DEPTH + 1], I32)
        over_e = sb("over_e", [P, TAB_BLOCKS])
        over_prev = sb("over_prev", [P, TAB_BLOCKS])
        over_i = sb("over_i", [P, TAB_BLOCKS], I32)
        over_r = sb("over_r", [P, TAB_BLOCKS])
        bidx = sb("bidx", [P, TAB_BLOCKS])

        landed = [sem(f"landed{s}") for s in range(SLOTS)]
        x_landed = sem("x_landed")
        pos_landed = sem("pos_landed")
        rows_landed = sem("rows_landed")
        router_landed = sem("router_landed")
        ws_landed = sem("ws_landed")
        gfin_landed = sem("gfin_landed")
        out_stored = sem("out_stored")

        zeroed = sem("zeroed")
        consts = sem("consts")
        passed = sem("passed")
        tri_done = sem("tri_done")
        pair_freed = sem("pair_freed")

        cols_ps = sem("cols_ps")
        hT_ps = sem("hT_ps")
        mixed = sem("mixed")
        idxT_ps = sem("idxT_ps")
        score_ps = sem("score_ps")
        qT_ps = sem("qT_ps")
        kT_ps = sem("kT_ps")
        logit_ps = sem("logit_ps")
        pT_ps = sem("pT_ps")
        ybT_ps = sem("ybT_ps")
        wsT_ps = sem("wsT_ps")
        vm_ps = sem("vm_ps")
        route_ps = sem("route_ps")
        rank_ps = sem("rank_ps")
        gather_ps = sem("gather_ps")
        selT_ps = sem("selT_ps")
        hidT_ps = sem("hidT_ps")
        scatter_ps = [sem(f"scatter_ps{t}") for t in range(NT)]

        ss_act = sem("ss_act")
        root = sem("root")
        xn_act = sem("xn_act")
        hT_act = sem("hT_act")
        high_act = sem("high_act")
        branch_act = sem("branch_act")
        merged_act = sem("merged_act")
        act_out = sem("act_out")
        idxT_act = sem("idxT_act")
        rel_act = sem("rel_act")
        qT_act = sem("qT_act")
        kT_act = sem("kT_act")
        exp_act = sem("exp_act")
        pT_act = sem("pT_act")
        ybT_act = sem("ybT_act")
        wsT_act = sem("wsT_act")
        route_exp = sem("route_exp")
        trig_act = sem("trig_act")
        selT_act = sem("selT_act")
        silu_act = sem("silu_act")
        hidT_act = sem("hidT_act")
        y_act = sem("y_act")

        setup_link = sem("setup_link")
        final_link = sem("final_link")
        dve_link = sem("dve_link")
        setup_done = sem("setup_done")
        layer_cols = sem("layer_cols")
        layer_params = sem("layer_params")
        inv_dve = sem("inv_dve")
        rstd_dve = sem("rstd_dve")
        xn_dve = sem("xn_dve")
        hT_dve = sem("hT_dve")
        low_dve = sem("low_dve")
        branch_low_dve = sem("branch_low_dve")
        merged_low_dve = sem("merged_low_dve")
        dve_out = sem("dve_out")
        idx_roped = sem("idx_roped")
        q_roped = sem("q_roped")
        k_roped = sem("k_roped")
        score_dve = sem("score_dve")
        exp_args = sem("exp_args")
        probs = sem("probs")
        v_normed = sem("v_normed")
        yaT_done = sem("yaT_done")
        ycT_done = sem("ycT_done")
        merged_done = sem("merged_done")
        route_args = sem("route_args")
        members = sem("members")
        pairs_known = sem("pairs_known")
        over_known = sem("over_known")
        sel_ready = sem("sel_ready")
        selw_ready = sem("selw_ready")
        xT_done = sem("xT_done")
        hid_done = sem("hid_done")
        y_dve = sem("y_dve")
        x_added = sem("x_added")
        final_done = sem("final_done")

        on_act = [n for n in range(N_RESULTS) if n <= G_U or G_GATE0 <= n < N_IN]
        on_dve = [n for n in range(N_RESULTS) if n not in on_act]

        block = ctx.enter_context(nc.Block())

        def alone(eng):
            eng.sem_inc(passed)

        def slot(s, n):
            return ring[:, s % SLOTS, 0:n]

        def unit_slots(unit):
            return [PAD + 2 * unit, PAD + 2 * unit + 1]

        def high_and_low(p):
            return [ring_parts[:, s, 0:words_of(p)] for s in (HIGH0 + p % HIGHS, mix_index(p))]

        def mix_slot(p):
            return ring[:, mix_index(p), 0:words_of(p)]


        def sync_program(sp):
            with nc.allow_non_contiguous_dma(reason="256 positions"):
                sp.dma_start(pos_i[:, :], positions.rearrange("a (t p) -> p (a t)", p=P)).then_inc(pos_landed, 16)
            for t in range(NT):
                sp.dma_start(x[:, t, :], x_in[0, t * P:(t + 1) * P, :]).then_inc(x_landed, 16)
            sp.dma_start(rows[0:DEPTH * KC, :], norm_mix_g.rearrange("l (c p) -> (l c) p", p=P)).then_inc(rows_landed, 16)
            sp.dma_start(rows[DEPTH * KC:, :], conv_w.rearrange("l k (c p) -> (l k c) p", p=P)).then_inc(rows_landed, 16)
            with sp.Fori(0, DEPTH) as l:
                if_known = l * 1 + 1
                sp.wait_ge(pairs_known, if_known)
                alone(sp)
                done = sp.value_load(pairs_i[0:1, bass.ds(l, 1)], min_val=0, max_val=DEPTH * MAX_PAIRS)

                def load(src, s, words):
                    dst = ring[:, s, 0:words]
                    if len(src.shape) == 3:
                        dst = dst.rearrange("p (c n) -> p c n", c=src.shape[1])
                    sp.dma_start(dst, src).then_inc(landed[s], 16)

                for p in range(PAD, MIX_SPAN):
                    if p - MIX_RING >= PAD:
                        sp.wait_ge(mixed, l * N_RESULTS + result_of(p - MIX_RING))
                    else:
                        sp.wait_ge(pair_freed, done * STAGES + 1 + mix_index(p) // QB)
                    alone(sp)
                    i = p - PAD
                    if i < 2 * N_IN:
                        g, half = i // 2, i % 2
                        n = N_IDX if g == G_QI else WB
                        src = w_in.rearrange("l (c p) n -> l p c n", p=P)[
                            bass.ds(l, 1), :, 4 * half:4 * half + 4, GROUPS[g]:GROUPS[g] + n]
                    elif i < 2 * N_IN + N_PROJ:
                        k = i - 2 * N_IN
                        w, half = (w_proj_a, w_proj_b, w_proj_c)[k % 3], k // 3
                        n = 512
                        src = w.rearrange("l (c p) n -> l p c n", p=P)[bass.ds(l, 1), :, :, 512 * half:512 * half + 512]
                    else:
                        part, half = (i - 2 * N_IN - N_PROJ) // 2, i % 2
                        assert P_OUT[part, half] == p
                        n = 512
                        src = w_out.rearrange("l (c p) n -> l p c n", p=P)[
                            bass.ds(l, 1), :, 4 * part:4 * part + 4, 512 * half:512 * half + 512]
                    load(src.rearrange("l p c n -> p (l c) n"), mix_index(p), 4 * n)
                    if i == 2 * G_CX:
                        sp.dma_start(ws_raw[:, :, :], gmlp_ws.rearrange("l g t s -> l t g s")[
                            bass.ds(l, 1)].rearrange("l t g s -> t (l g) s")).then_inc(ws_landed, 16)
                        sp.dma_start(bs_row[0:1, :], gmlp_b.rearrange("l g t -> l (g t)")[
                            bass.ds(l, 1)]).then_inc(ws_landed, 16)

                def load_pair(g, experts):
                    for p in range(PAIR_SLOTS):
                        k, j = p // QB, p % QB
                        sp.wait_ge(mixed, l * N_RESULTS + mixing_reader(p))
                        alone(sp)
                        if j == 0:
                            sp.wait_ge(pair_freed, g * STAGES + 1 + k)
                            alone(sp)
                        e = experts[j]
                        if k < 4:
                            w = (expert_w_gate, expert_w_up)[k % 2]
                            src = w.rearrange("l e (p c) n -> (l e) p (c n)", c=KC)[
                                bass.ds(e, 1), :, SLOT * (k // 2):SLOT * (k // 2 + 1)]
                        else:
                            src = expert_w_down.rearrange("l e (p c) n -> (l e) p (c n)", c=FC)[
                                bass.ds(e, 1), :, SLOT * (k - 4):SLOT * (k - 3)]
                        load(src.rearrange("e p n -> (e p) n"), p, SLOT)

                with sp.Fori(0, MAIN_PAIRS) as i:
                    load_pair(done + i, [l * NE + i * QB + j for j in range(QB)])
                sp.wait_ge(pairs_known, l + 2)
                sp.wait_ge(over_known, l + 1)
                alone(sp)
                end = sp.value_load(pairs_i[0:1, bass.ds(l + 1, 1)], min_val=MAIN_PAIRS, max_val=DEPTH * MAX_PAIRS)
                with sp.If(end > done + MAIN_PAIRS):
                    with sp.Fori(0, nc.s_assert_within(end - done - MAIN_PAIRS, 0, OVER_BLOCKS // QB)) as i:
                        experts = [sp.value_load(over_i[0:1, bass.ds(i * QB + j, 1)], min_val=0, max_val=NE - 1)
                                   for j in range(QB)]
                        load_pair(done + MAIN_PAIRS + i, [l * NE + e for e in experts])
            sp.wait_ge(merged_done, 2 * DEPTH)
            sp.dma_start(gfin[:, :], norm_final_g.rearrange("(a d) -> a d", a=1).to_broadcast([P, D])).then_inc(gfin_landed, 16)
            for t in range(NT):
                sp.wait_ge(final_done, t + 1)
                sp.dma_start(out[0, t * P:(t + 1) * P, :], xn[:, t * D:(t + 1) * D]).then_inc(out_stored, 16)
            sp.wait_ge(out_stored, 16 * NT)

        def router_loads(act):
            with nc.allow_non_contiguous_dma(reason="a few gains"):
                act.dma_start(g_ffn_all[:, :, :], norm_ffn_g.rearrange("l (p c) -> p l c", c=KC)).then_inc(router_landed, 16)
                act.dma_start(rg_all[:, :, :, :].rearrange("p l c n -> p l (c n)"),
                              router_group_w.rearrange("l (p c) n -> p l (c n)", c=KC)).then_inc(router_landed, 16)
                act.dma_start(re_all[:, :, :, :].rearrange("p l c n -> p l (c n)"),
                              router_expert_w.rearrange("l (p c) n -> p l (c n)", c=KC)).then_inc(router_landed, 16)
                act.dma_start(rgb_all[:, :, :].rearrange("p l n -> p (l n)"),
                              router_group_b.rearrange("(a l) n -> a (l n)", a=1).to_broadcast([P, DEPTH * NG])).then_inc(router_landed, 16)
                act.dma_start(reb_all[:, :, :].rearrange("p l n -> p (l n)"),
                              router_expert_b.rearrange("(a l) n -> a (l n)", a=1).to_broadcast([P, DEPTH * NE])).then_inc(router_landed, 16)

        def pool_program(pool):
            gp = nc.gpsimd
            gp.memset(ident[:, :], 0.0).then_inc(zeroed, 1)
            gp.memset(before[:, :], 0.0).then_inc(zeroed, 1)
            gp.memset(causal[:, :], 0.0).then_inc(zeroed, 1)
            gp.memset(ones[:, :], 1.0)
            gp.memset(z[:, :, :], 0.0)
            gp.memset(cumA[:, :], 0.0)
            gp.memset(cumB[:, :], 0.0)
            gp.memset(glog[:, :, :], TAKEN)
            for j in range(ROT):
                gp.memset(inv_freq[:, j:j + 1], float(np.float32(ROPE_THETA) ** np.float32(-j * 2.0 / (2 * ROT))))
            gp.iota(slots1[:, :], pattern=[[1, BLK]], base=1, channel_multiplier=0, allow_small_or_imprecise_dtypes=True)
            gp.iota(iota[:, :], pattern=[[1, NE]], base=0, channel_multiplier=0, allow_small_or_imprecise_dtypes=True)
            gp.iota(bidx[:, :], pattern=[[1, TAB_BLOCKS]], base=0, channel_multiplier=0, allow_small_or_imprecise_dtypes=True)
            gp.iota(thresholds[:, :], pattern=[[BLK, S // BLK - 1]], base=BLK, channel_multiplier=0, allow_small_or_imprecise_dtypes=True)
            pool.wait_ge(zeroed, 3)
            gp.affine_select(out=ident[:, :], in_=ident[:, :], compare_op=ALU.not_equal, fill=1.0, base=0,
                             pattern=[[-1, P]], channel_multiplier=1).then_inc(consts, 1)
            gp.affine_select(out=before[:, :], in_=before[:, :], compare_op=ALU.is_ge, fill=1.0, base=0,
                             pattern=[[-1, P]], channel_multiplier=1).then_inc(consts, 1)
            gp.affine_select(out=causal[:, :], in_=causal[:, :], compare_op=ALU.is_ge, fill=NEG, base=P,
                             pattern=[[-1, S]], channel_multiplier=1).then_inc(consts, 1)
            for k in range(STAGES):
                gp.memset(credit[:, k:k + 1], 0.0).then_inc(pair_freed, 1)
            with pool.Fori(0, DEPTH) as l:
                pool.wait_ge(wsT_act, l + 1)
                alone(pool)
                gp.affine_select(out=wsT[:, :, :], in_=wsT[:, :, :], compare_op=ALU.is_ge, fill=0.0, base=0,
                                 pattern=[[0, HEADS], [1, P]], channel_multiplier=-1).then_inc(tri_done, 1)

        def scalar_program(act):
            sc = nc.scalar
            router_loads(act)
            act.wait_ge(setup_link, TRIG_READY)
            sc.activation(sin[:, :, :], ang[:, 0], ACT.Sin)
            sc.activation(cos[:, :, :], ang[:, 1], ACT.Sin).then_inc(trig_act, 1)

            def sqrt_table():
                sc.activation(spare[:, :], ones[:, 0:1], ACT.Sqrt)

            with act.Fori(0, DEPTH) as l:
                act.wait_ge(pairs_known, l + 1)
                alone(act)
                start = act.value_load(pairs_i[0:1, bass.ds(l, 1)], min_val=0, max_val=DEPTH * MAX_PAIRS)

                def even_bank(ps, b, dst, gain):
                    for c in range(2):
                        ins = sc.activation(dst[:, 2 * b + c, :], ps[:, b % 2, c * S:(c + 1) * S], ACT.Copy,
                                            scale=gain[:, 2 * b + c:2 * b + c + 1])
                    ins.then_inc(hT_act, 1)

                def mixing_norm():
                    sqrt_table()
                    act.wait_ge(x_landed, 16 * NT)
                    act.wait_ge(x_added, start * 2 + 1)
                    sc.activation(xn[:, 0:D], x[:, 0, :], ACT.Square, accum_out=ss[:, 0:1]).then_inc(ss_act, 1)
                    root_of(0)
                    high(unit_slots(0)[0])
                    act.wait_ge(rstd_dve, l * 2 + 1)
                    sc.activation(xn[:, 0:D], x[:, 0, :], ACT.Copy, scale=rstd[:, 0:1]).then_inc(xn_act, 1)
                    high(unit_slots(0)[1])
                    act.wait_ge(layer_cols, l + 1)
                    for b in range(4):
                        act.wait_ge(hT_ps, l * 8 + b + 1)
                        even_bank((psA, psB)[b // 2], b, hT_high, g_mix)

                def router_norm():
                    sqrt_table()
                    act.wait_ge(dve_out, (l + 1) * len(on_dve))
                    sc.activation(xn[:, 0:D], x[:, 0, :], ACT.Square, accum_out=ss[:, 0:1]).then_inc(ss_act, 1)
                    act.wait_ge(layer_params, l + 1)
                    act.wait_ge(hT_ps, l * 8 + 5)
                    even_bank(psA, 0, hT, g_ffn)
                    root_of(2)
                    act.wait_ge(hT_ps, l * 8 + 7)
                    even_bank(psB, 2, hT, g_ffn)
                    act.wait_ge(rstd_dve, l * 2 + 2)
                    for t in range(NT):
                        ins = sc.activation(xn[:, t * D:(t + 1) * D].rearrange("p (c q) -> p c q", c=KC),
                                            x[:, t, :].rearrange("p (q c) -> p c q", c=KC), ACT.Copy, scale=rstd[:, t:t + 1])
                    ins.then_inc(xn_act, 1)

                def high(*ps):
                    for p in ps:
                        s = mix_index(p)
                        k = sum(1 for q in range(PAD, p + 1) if mix_index(q) == s)
                        act.wait_ge(landed[s], l * (16 * MIX_USES[s]) + start * 16 + 16 * k)
                        if p - HIGHS >= PAD:
                            act.wait_ge(mixed, l * N_RESULTS + result_of(p - HIGHS))
                        sc.activation(high_and_low(p)[0], mix_slot(p), ACT.Copy).then_inc(high_act, 1)

                def root_of(n):
                    act.wait_ge(inv_dve, l * 3 + n + 1)
                    sc.activation(rstd[:, :], inv[:, :], ACT.Sqrt).then_inc(root, 1)

                def merged_part(half):
                    act.wait_ge(merged_done, l * 2 + half + 1)
                    sc.activation(merged_high[:, 4 * half:4 * half + 4, :], merged[:, 4 * half:4 * half + 4, :],
                                  ACT.Copy).then_inc(merged_act, 1)

                def result(n):
                    act.wait_ge(mixed, l * N_RESULTS + n + 1)
                    return (psA, psB)[n % 2]

                mixing_norm()
                high(*unit_slots(1))
                ps = result(G_QI)
                sc.activation(idx[:, :, 0:320], ps[:, :, 0:320], ACT.Copy)
                sc.activation(idx[:, :, 384:388], ps[:, :, 320:324], ACT.Copy).then_inc(act_out, 1)
                high(*unit_slots(2))
                sc.activation(q_tok, result(G_Q)[:, :, :], ACT.Copy).then_inc(act_out, 1)
                act.wait_ge(idxT_ps, l + 1)
                sc.activation(qiT[:, :, :], psC[:, 0, :].rearrange("p (a s) -> p a s", a=2), ACT.Copy)
                sc.activation(kiT[:, :], psC[:, 1, 0:S], ACT.Copy).then_inc(idxT_act, 1)
                high(*unit_slots(3))
                sc.activation(k_tok, result(G_K)[:, :, :], ACT.Copy).then_inc(act_out, 1)
                high(unit_slots(4)[0])
                act.wait_ge(score_ps, l * 2 + 1)
                for r in range(2):
                    ins = sc.activation(p0[:, r::2, :], psD[:, r, 0:S].rearrange("p (a s) -> p a s", a=2), ACT.Relu, scale=IDX_SCALE)
                ins.then_inc(rel_act, 1)
                act.wait_ge(score_ps, l * 2 + 2)
                for r in range(2):
                    ins = sc.activation(rel[:, r::2, :], psC[:, r, :].rearrange("p (a s) -> p a s", a=2), ACT.Relu, scale=IDX_SCALE)
                ins.then_inc(rel_act, 1)
                high(unit_slots(4)[1])
                sc.activation(v_tok, result(G_V)[:, :, :], ACT.Copy).then_inc(act_out, 1)
                high(*unit_slots(5))
                act.wait_ge(qT_ps, l + 1)
                sc.activation(qT.rearrange("p (b h) s -> p b (h s)", b=2), psD[:, :, :], ACT.Copy).then_inc(qT_act, 1)
                sc.activation(vg[:, :, :], result(G_VA)[:, :, :], ACT.Gelu_apprx_tanh).then_inc(act_out, 1)
                high(*unit_slots(6))
                act.wait_ge(kT_ps, l + 1)
                sc.activation(kT.rearrange("p (b h) s -> p b (h s)", b=2), psC[:, :, :], ACT.Copy).then_inc(kT_act, 1)
                sc.activation(uT[:, :, :].rearrange("p (b h) s -> p b (h s)", b=2), result(G_U)[:, :, :],
                              ACT.Gelu_apprx_tanh).then_inc(act_out, 1)
                high(*unit_slots(7))
                for b, pr, nk in ((0, p0, P), (1, rel, S)):
                    act.wait_ge(exp_args, l * 2 + b + 1)
                    for h in range(HEADS):
                        ins = sc.activation(pr[:, h, 0:nk], pr[:, h, 0:nk], ACT.Exp, bias=mx[:, b, h:h + 1],
                                            accum_out=den[:, b, h:h + 1])
                    ins.then_inc(exp_act, 1)
                root_of(1)
                high(*unit_slots(8))
                high(*unit_slots(9))
                act.wait_ge(pT_ps, l * 2 + 2)
                sc.activation(pT[:, 0, :, :].rearrange("p h q -> p (h q)"), psD[:, 1, :], ACT.Copy)
                sc.activation(pT[:, 1:3, :, :].rearrange("p k h q -> p k (h q)"), psC[:, :, :], ACT.Copy).then_inc(pT_act, 1)
                high(*unit_slots(10))
                act.wait_ge(ybT_ps, l + 1)
                sc.activation(ybT[:, :, :].rearrange("p (b h) s -> p b (h s)", b=2), psD[:, :, :], ACT.Copy).then_inc(ybT_act, 1)
                act.wait_ge(wsT_ps, l + 1)
                sc.activation(wsT[:, :, :].rearrange("p h s -> p (h s)"), psC[:, 0, :], ACT.Copy).then_inc(wsT_act, 1)
                act.wait_ge(dve_out, l * len(on_dve) + 1 + on_dve.index(G_CB))
                sc.activation(branch_high[2][:, :, :], ycT[:, :, :], ACT.Copy).then_inc(branch_act, 1)
                for n in range(6):
                    sc.activation(gates[:, n].rearrange("p (b h) s -> p b (h s)", b=2), result(G_GATE0 + n)[:, :, :],
                                  ACT.Sigmoid).then_inc(act_out, 1)
                    if n == 2:
                        act.wait_ge(yaT_done, l + 1)
                        sc.activation(ya_high, uT[:, :, :], ACT.Copy).then_inc(branch_act, 1)
                    high(*unit_slots(G_GATE0 + n + 2))
                high(*unit_slots(17))
                merged_part(0)
                high(*unit_slots(18))
                high(*unit_slots(19))
                merged_part(1)

                router_norm()
                act.wait_ge(route_args, l + 1)
                sc.activation(ex[:, :, :], ex[:, :, :], ACT.Exp).then_inc(route_exp, 1)

                act.wait_ge(pairs_known, l + 2)
                alone(act)
                end = act.value_load(pairs_i[0:1, bass.ds(l + 1, 1)], min_val=MAIN_PAIRS, max_val=DEPTH * MAX_PAIRS)
                with act.Fori(start, end) as g:
                    act.wait_ge(selT_ps, g + 1)
                    sc.activation(selwT.rearrange("p t n -> p (t n)"), psD[:, 1, 0:S], ACT.Copy).then_inc(selT_act, 1)
                    act.wait_ge(pair_freed, g * STAGES + STAGES + 3)
                    sc.activation(silu, psB[:, 0, :], ACT.Silu).then_inc(silu_act, 1)
                    act.wait_ge(hidT_ps, g + 1)
                    sc.activation(hidT.rearrange("p c n -> p (c n)"), psD[:, 0, :], ACT.Copy).then_inc(hidT_act, 1)
                    act.wait_ge(pair_freed, g * STAGES + 2 * STAGES)
                    sc.activation(y[:, 0, :], psC[:, 0, :], ACT.Copy).then_inc(y_act, 1)

            act.wait_ge(pairs_known, DEPTH + 1)
            last = act.value_load(pairs_i[0:1, DEPTH:DEPTH + 1], min_val=MAIN_PAIRS, max_val=DEPTH * MAX_PAIRS)
            sqrt_table()
            act.wait_ge(x_added, last * 2)
            sc.activation(xn[:, 0:D], x[:, 0, :], ACT.Square, accum_out=ss[:, 0:1]).then_inc(ss_act, 1)
            act.wait_ge(inv_dve, 3 * DEPTH + 1)
            sc.activation(rstd[:, :], inv[:, :], ACT.Sqrt).then_inc(root, 1)

        def vector_program(dve):
            v = nc.vector
            count = [0]

            def setup(ins):
                count[0] += 1
                ins.then_inc(setup_link, 1)
                dve.wait_ge(setup_link, count[0])

            setup(v.memset(pairs_f[:, :], 0.0))
            v.memset(pairs_i[:, :], 0).then_inc(pairs_known, 1)
            v.memset(total[:, :], 0.0).then_inc(x_added, 1)
            dve.wait_ge(pos_landed, 16)
            dve.wait_ge(consts, 3)
            setup(v.tensor_copy(pos_f[:, :], pos_i[:, :]))
            for t in range(NT):
                ins = v.tensor_scalar(ang[:, 2, t, :], inv_freq[:, :], pos_f[:, t:t + 1], None, ALU.mult)
            setup(ins)
            setup(v.tensor_scalar(ang[:, 1], ang[:, 2], 1.0 / TWO_PI, ROUND_MAGIC, ALU.mult, ALU.add))
            setup(v.tensor_scalar(ang[:, 1], ang[:, 1], ROUND_MAGIC, None, ALU.subtract))
            setup(v.scalar_tensor_tensor(ang[:, 2], ang[:, 1], -TWO_PI_HI, ang[:, 2], ALU.mult, ALU.add))
            setup(v.scalar_tensor_tensor(ang[:, 2], ang[:, 1], -TWO_PI_MID, ang[:, 2], ALU.mult, ALU.add))
            setup(v.scalar_tensor_tensor(ang[:, 2], ang[:, 1], -TWO_PI_LO, ang[:, 2], ALU.mult, ALU.add))
            lim = float(np.nextafter(np.float32(np.pi), np.float32(0)))
            setup(v.tensor_scalar(ang[:, 0], ang[:, 2], lim, -lim, ALU.min, ALU.max))
            setup(v.scalar_tensor_tensor(ang[:, 1], ang[:, 0], -1.0, ang[:, 0], ALU.mult, ALU.max))
            setup(v.tensor_scalar(ang[:, 1], ang[:, 1], -1.0, float(np.pi / 2), ALU.mult, ALU.add))
            assert count[0] == TRIG_READY
            v.tensor_copy(before_r[:, :], before[:, :])
            v.tensor_copy(ones_r[:, :], ones[:, :])
            dve.wait_ge(cols_ps, 1)
            v.tensor_copy(cols[:, :], psD[:, 1, 0:cols.shape[1]]).then_inc(setup_done, 1)
            dve.wait_ge(setup_done, 1)

            def variance(src, scale, step):
                step(v.tensor_scalar(var[:, :], src, scale, EPS, ALU.mult, ALU.add))
                v.reciprocal(inv[:, :], var[:, :]).then_inc(inv_dve, 1)

            def newton_step(n, step):
                dve.wait_ge(root, n)
                step(v.tensor_tensor(newton[:, :], rstd[:, :], rstd[:, :], ALU.mult))
                step(v.tensor_tensor(newton[:, :], newton[:, :], var[:, :], ALU.mult))
                step(v.tensor_scalar(newton[:, :], newton[:, :], -0.5, 1.5, ALU.mult, ALU.add))
                return v.tensor_tensor(rstd[:, :], rstd[:, :], newton[:, :], ALU.mult)

            with dve.Fori(0, DEPTH) as l:
                linked = [0]

                def link(ins, wait_alone=False):
                    linked[0] += 1
                    ins.then_inc(dve_link, 1)
                    dve.wait_ge(dve_link, l * DVE_MIX + linked[0])
                    if wait_alone:
                        alone(dve)

                def low(*ps):
                    for p in ps:
                        dve.wait_ge(high_act, l * MIX_SLOTS + p - PAD + 1)
                        high_part, low_part = high_and_low(p)
                        v.tensor_tensor(low_part, mix_slot(p), high_part, ALU.subtract).then_inc(low_dve, 1)

                def parameters():
                    v.tensor_copy(g_mix[:, :], cols[:, bass.ds(l * KC, KC)]).then_inc(layer_cols, 1)
                    v.tensor_copy(w_conv[:, :], cols[:, bass.ds(l * (4 * CONV) + DEPTH * KC, 4 * CONV)])
                    dve.wait_ge(router_landed, 16 * 5)
                    v.tensor_copy(g_ffn[:, :], g_ffn_all[:, bass.ds(l, 1), :].rearrange("p l c -> p (l c)"))
                    v.tensor_copy(r_w[:, :, 0:NG], rg_all[:, bass.ds(l, 1), :, :].rearrange("p l c n -> p (l c) n"))
                    v.tensor_copy(r_w[:, :, NG:], re_all[:, bass.ds(l, 1), :, :].rearrange("p l c n -> p (l c) n"))
                    v.tensor_copy(r_b[:, 0:NG], rgb_all[:, bass.ds(l, 1), :].rearrange("p l n -> p (l n)"))
                    v.tensor_copy(r_b[:, NG:], reb_all[:, bass.ds(l, 1), :].rearrange("p l n -> p (l n)")).then_inc(layer_params, 1)

                def squares(which):
                    link(v.tensor_tensor_reduce(xn[:, D:2 * D], x[:, 1, :], x[:, 1, :], 1.0, 0.0, ALU.mult, ALU.add, ss[:, 1:2]))
                    dve.wait_ge(ss_act, l * 2 + which + 1)
                    variance(ss[:, :], 1.0 / D, link)

                def mixing_norm():
                    squares(0)
                    newton_step(l * 3 + 1, link).then_inc(rstd_dve, 1)
                    dve.wait_ge(rstd_dve, l * 2 + 1)
                    v.tensor_scalar(xn[:, D:2 * D], x[:, 1, :], rstd[:, 1:2], None, ALU.mult).then_inc(xn_dve, 1)
                    parameters()
                    dve.wait_ge(layer_params, l + 1)
                    low(*unit_slots(0))
                    for b in range(4):
                        dve.wait_ge(hT_act, l * 6 + b + 1)
                        for c in range(2):
                            m = 2 * b + c
                            ins = v.scalar_tensor_tensor(hT_low[:, m, :], (psA, psB)[b // 2][:, b % 2, c * S:(c + 1) * S],
                                                         g_mix[:, m:m + 1], hT_high[:, m, :], ALU.mult, ALU.subtract)
                        ins.then_inc(hT_dve, 1)
                    low(*unit_slots(1))

                def router_norm():
                    squares(1)
                    for b, ps in ((1, psA), (3, psB)):
                        dve.wait_ge(hT_ps, l * 8 + 5 + b)
                        v.tensor_tensor(hT[:, 2 * b:2 * b + 2, :], ps[:, 1, :].rearrange("p (c s) -> p c s", c=2),
                                        g_ffn[:, 2 * b:2 * b + 2].unsqueeze(2).to_broadcast([P, 2, S]), ALU.mult).then_inc(hT_dve, 1)
                    newton_step(l * 3 + 3, link).then_inc(rstd_dve, 1)
                    dve.wait_ge(rstd_dve, l * 2 + 2)

                def result(n):
                    dve.wait_ge(mixed, l * N_RESULTS + n + 1)
                    return (psA, psB)[n % 2]

                dve.wait_ge(x_landed, 16 * NT)
                mixing_norm()

                def rope(view, cos_t, sin_t, heads, half):
                    n = NT * heads * half
                    t4 = [tmp[:, i * n:(i + 1) * n].rearrange("p (t h i) -> p t h i", t=NT, h=heads) for i in range(4)]
                    x1, x2 = view[:, :, :, 0:half], view[:, :, :, half:2 * half]
                    cb = cos_t.unsqueeze(2).to_broadcast([P, NT, heads, half])
                    sb_ = sin_t.unsqueeze(2).to_broadcast([P, NT, heads, half])
                    v.tensor_tensor(t4[0], x1, cb, ALU.mult)
                    v.tensor_tensor(t4[1], x2, sb_, ALU.mult)
                    v.tensor_tensor(t4[2], x1, sb_, ALU.mult)
                    link(v.tensor_tensor(t4[3], x2, cb, ALU.mult))
                    v.tensor_tensor(x1, t4[0], t4[1], ALU.subtract)
                    return v.tensor_tensor(x2, t4[2], t4[3], ALU.add)

                dve.wait_ge(act_out, l * len(on_act) + 1 + on_act.index(G_QI))
                dve.wait_ge(trig_act, 1)
                heads5 = idx[:, :, 0:320].rearrange("p t (h w) -> p t h w", h=IH + 1)
                link(rope(heads5, cos[:, :, 0::2], sin[:, :, 0::2], IH + 1, IROT))
                v.tensor_scalar(wi[:, :, :], idx[:, :, 384:388], IDX_W_SCALE, None, ALU.mult)
                v.tensor_copy(idx[:, :, 320:384], idx[:, :, 256:320]).then_inc(idx_roped, 1)
                low(*unit_slots(2))
                dve.wait_ge(act_out, l * len(on_act) + 1 + on_act.index(G_Q))
                rope(q_tok.rearrange("p t (h w) -> p t h w", h=HEADS), cos[:, :, :], sin[:, :, :], HEADS, ROT).then_inc(q_roped, 1)
                low(*unit_slots(3))
                dve.wait_ge(act_out, l * len(on_act) + 1 + on_act.index(G_K))
                dve.wait_ge(q_roped, l + 1)
                rope(k_tok.rearrange("p t (h w) -> p t h w", h=HEADS), cos[:, :, :], sin[:, :, :], HEADS, ROT).then_inc(k_roped, 1)
                low(*unit_slots(4))

                for b, terms, nk in ((0, p0, P), (1, rel, S)):
                    limit = causal[:, S - nk:S]
                    dve.wait_ge(rel_act, l * 2 + b + 1)
                    for h in range(IH):
                        link(v.scalar_tensor_tensor(score[:, 0:nk], terms[:, h, 0:nk], wi[:, b, h:h + 1],
                                                    limit if h == 0 else score[:, 0:nk], ALU.mult, ALU.add), h == IH - 1)
                    for r in range(TOPK // 8):
                        left = score if r == 0 else work
                        link(v.max(top8[:, :], left[:, 0:nk]), True)
                        link(v.match_replace(work[:, 0:nk], top8[:, :], left[:, 0:nk], TAKEN), r < TOPK // 8 - 1)
                    link(v.tensor_tensor(maskb[:, b, 0:nk], work[:, 0:nk], score[:, 0:nk], ALU.is_equal))
                    link(v.scalar_tensor_tensor(maskb[:, b, 0:nk], maskb[:, b, 0:nk], NEG, limit, ALU.mult, ALU.add))
                    if b == 0:
                        low(*unit_slots(5))

                dve.wait_ge(act_out, l * len(on_act) + 1 + on_act.index(G_VA))
                for t in range(NT):
                    ins = v.bn_stats(stats[:, t, :], vg[:, t, :])
                link(ins, True)
                for t in range(NT):
                    ins = v.bn_aggr(mv[:, t, :], stats[:, t, :])
                link(ins)
                variance(mv[:, :, 1], 1.0, link)
                low(*unit_slots(6))

                for b, pr, nk in ((0, p0, P), (1, rel, S)):
                    dve.wait_ge(logit_ps, l * 2 + b + 1)
                    if b == 0:
                        src = psD[:, 0, :].rearrange("p (h s) -> p h s", h=HEADS)
                        link(v.scalar_tensor_tensor(pr[:, :, 0:nk], src, LOGIT_SCALE,
                                                    maskb[:, b:b + 1, 0:nk].to_broadcast([P, HEADS, nk]), ALU.mult, ALU.add))
                    else:
                        for r in range(2):
                            src = psC[:, r, :].rearrange("p (h s) -> p h s", h=2)
                            ins = v.scalar_tensor_tensor(pr[:, 2 * r:2 * r + 2, 0:nk], src, LOGIT_SCALE,
                                                         maskb[:, b:b + 1, 0:nk].to_broadcast([P, 2, nk]), ALU.mult, ALU.add)
                        link(ins)
                    link(v.tensor_reduce(mx[:, b, :], pr[:, :, 0:nk], AX.X, ALU.max))
                    v.tensor_scalar(mx[:, b, :], mx[:, b, :], -1.0, None, ALU.mult).then_inc(exp_args, 1)

                low(*unit_slots(7))
                zz = z[:, :, CONV - 1:].rearrange("p (b m) s -> p b m s", b=2)
                v.tensor_copy(zz, result(G_CX)[:, :, :].rearrange("p b (m s) -> p b m s", m=2)).then_inc(dve_out, 1)
                dve.wait_ge(dve_out, l * len(on_dve) + 1 + on_dve.index(G_CX))

                for b, pr, nk in ((0, p0, P), (1, rel, S)):
                    dve.wait_ge(exp_act, l * 2 + b + 1)
                    link(v.reciprocal(rden[:, b, :], den[:, b, :]))
                    v.tensor_tensor(pr[:, :, 0:nk], pr[:, :, 0:nk],
                                    rden[:, b, :].unsqueeze(2).to_broadcast([P, HEADS, nk]), ALU.mult).then_inc(probs, 1)

                low(*unit_slots(8))
                link(newton_step(l * 3 + 2, link))
                for t in range(NT):
                    ins = v.tensor_scalar(vg[:, t, :], vg[:, t, :], mv[:, t, 0:1], rstd[:, t:t + 1], ALU.subtract, ALU.mult)
                ins.then_inc(v_normed, 1)

                ps = result(G_CC)
                v.tensor_tensor(zz, ps[:, :, :].rearrange("p b (m s) -> p b m s", m=2), zz, ALU.mult).then_inc(dve_out, 1)
                dve.wait_ge(dve_out, l * len(on_dve) + 1 + on_dve.index(G_CC))
                low(*unit_slots(9))
                yc = tmp[:, :].rearrange("p (m s) -> p m s", m=4)
                for k in range(CONV):
                    for m in range(4):
                        wk = w_conv[:, k * 4 + m:k * 4 + m + 1]
                        if k == 0:
                            ins = v.tensor_scalar(yc[:, m, :], z[:, m, 0:S], wk, None, ALU.mult)
                        else:
                            ins = v.scalar_tensor_tensor(yc[:, m, :], z[:, m, k:k + S], wk, yc[:, m, :], ALU.mult, ALU.add)
                    link(ins)
                ps = result(G_CB)
                v.tensor_tensor(ycT[:, :, :].rearrange("p (b m) s -> p b (m s)", b=2), ps[:, :, :],
                                tmp[:, :].rearrange("p (b n) -> p b n", b=2), ALU.mult).then_inc(dve_out, 1)
                low(*unit_slots(10))
                dve.wait_ge(ybT_act, l + 1)
                v.tensor_tensor(yb_low.rearrange("p (b h) s -> p b (h s)", b=2), psD[:, :, :],
                                ybT[:, :, :].rearrange("p (b h) s -> p b (h s)", b=2), ALU.subtract).then_inc(branch_low_dve, 1)
                dve.wait_ge(branch_act, l * 2 + 1)
                v.tensor_tensor(branch_low[2][:, :, :], ycT[:, :, :], branch_high[2][:, :, :], ALU.subtract).then_inc(branch_low_dve, 1)
                low(*unit_slots(11))

                dve.wait_ge(pairs_known, l + 1)
                alone(dve)
                start = dve.value_load(pairs_i[0:1, bass.ds(l, 1)], min_val=0, max_val=DEPTH * MAX_PAIRS)
                dve.wait_ge(vm_ps, l + 1)
                dve.wait_ge(act_out, l * len(on_act) + 1 + on_act.index(G_U))
                uu = uT[:, :, :].rearrange("p (b h) s -> p b (h s)", b=2)
                v.tensor_tensor(uu, uu, psC[:, :, :], ALU.mult).then_inc(yaT_done, 1)
                low(*unit_slots(12))
                dve.wait_ge(branch_act, l * 2 + 2)
                v.tensor_tensor(branch_low[0][:, :, :], uT[:, :, :], ya_high, ALU.subtract).then_inc(branch_low_dve, 1)
                for unit in range(13, 17):
                    low(*unit_slots(unit))

                def merged_part(half):
                    dve.wait_ge(merged_act, l * 2 + half + 1)
                    part = slice(4 * half, 4 * half + 4)
                    v.tensor_tensor(merged_low[:, part, :], merged[:, part, :], merged_high[:, part, :],
                                    ALU.subtract).then_inc(merged_low_dve, 1)

                dve.wait_ge(act_out, (l + 1) * len(on_act))
                for half in range(2):
                    dst = merged[:, 4 * half:4 * half + 4, :].rearrange("p (b h) s -> p b (h s)", b=2)
                    t2 = tmp[:, :].rearrange("p (b n) -> p b n", b=2)
                    for branch in range(3):
                        n = N_IN + 3 * half + branch
                        gate = gates[:, 2 * branch + half].rearrange("p (b h) s -> p b (h s)", b=2)
                        v.tensor_tensor(dst if branch == 0 else t2, result(n)[:, :, :], gate, ALU.mult).then_inc(dve_out, 1)
                        dve.wait_ge(dve_out, l * len(on_dve) + 1 + on_dve.index(n))
                        if branch:
                            ins = v.tensor_tensor(dst, dst, t2, ALU.add)
                        if branch == 1:
                            link(ins)
                        if n == N_IN + 1:
                            low(*unit_slots(17))
                        if n == N_IN + 3:
                            merged_part(0)
                            low(*unit_slots(18))
                    ins.then_inc(merged_done, 1)
                    dve.wait_ge(merged_done, l * 2 + half + 1)
                low(*unit_slots(19))
                merged_part(1)
                for half in range(2):
                    n = N_IN + N_PROJ + half
                    dst = x[:, :, 512 * half:512 * half + 512]
                    v.tensor_tensor(dst, dst, result(n)[:, :, :], ALU.add).then_inc(dve_out, 1)
                dve.wait_ge(dve_out, (l + 1) * len(on_dve))

                router_norm()
                dve.wait_ge(route_ps, l + 1)
                lg = psC[:, :, 0:N_ROUTE]
                for t in range(NT):
                    v.scalar_tensor_tensor(elog[:, t].rearrange("p g e -> p (g e)"), lg[:, t, NG:], rstd[:, t:t + 1],
                                           r_b[:, NG:], ALU.mult, ALU.add)
                for t in range(NT):
                    ins = v.scalar_tensor_tensor(glog[:, t, 0:NG], lg[:, t, 0:NG], rstd[:, t:t + 1], r_b[:, 0:NG], ALU.mult, ALU.add)
                link(ins, True)
                for t in range(NT):
                    ins = v.max(gtop[:, t, :], glog[:, t, :])
                link(ins, True)
                for t in range(NT):
                    ins = v.max_index(gtop_i[:, t, :], gtop[:, t, :], glog[:, t, :])
                link(ins)
                v.tensor_tensor(ex[:, :, 0:NG], glog[:, :, 0:NG], gtop[:, :, 0:1].to_broadcast([P, NT, NG]), ALU.subtract)
                link(v.tensor_copy(gidx[:, :], gtop_i[:, :, 0]))
                for t in range(NT):
                    ins = v.tensor_scalar(gpen[:, t, :], iota[:, 0:NG], gidx[:, t:t + 1], NEG, ALU.not_equal, ALU.mult)
                link(ins)
                link(v.tensor_tensor(em[:, :, :, :].rearrange("p t g e -> p (t g) e"), elog[:, :, :, :].rearrange("p t g e -> p (t g) e"),
                                     gpen[:, :, :].rearrange("p t g -> p (t g)").unsqueeze(2).to_broadcast([P, NT * NG, EPG]),
                                     ALU.add), True)
                for t in range(NT):
                    ins = v.max(etop[:, t, :], em[:, t].rearrange("p g e -> p (g e)"))
                link(ins, True)
                for t in range(NT):
                    ins = v.max_index(etop_i[:, t, :], etop[:, t, :], em[:, t].rearrange("p g e -> p (g e)"))
                link(ins)
                v.tensor_tensor(ex[:, :, NG:NG + 1], etop[:, :, 1:2], etop[:, :, 0:1], ALU.subtract).then_inc(route_args, 1)
                link(v.tensor_copy(eidx[:, :, :], etop_i[:, :, 0:2]))
                for k, oh in ((0, oh0), (1, oh1)):
                    ins = v.tensor_tensor(oh[:, :, :], iota[:, :].unsqueeze(1).to_broadcast([P, NT, NE]),
                                          eidx[:, :, k:k + 1].to_broadcast([P, NT, NE]), ALU.is_equal)
                link(ins)
                v.tensor_tensor(member[:, :, :], oh0[:, :, :], oh1[:, :, :], ALU.add).then_inc(members, 1)
                dve.wait_ge(route_exp, l + 1)
                link(v.tensor_reduce(gsum[:, :], ex[:, :, 0:NG], AX.X, ALU.add))
                link(v.scalar_tensor_tensor(tw[:, :, 1:2], ex[:, :, NG:NG + 1], 1.0, gsum[:, :].unsqueeze(2), ALU.add, ALU.mult))
                link(v.reciprocal(tw[:, :, 0:1], tw[:, :, 1:2]))
                link(v.tensor_tensor(tw[:, :, 1:2], tw[:, :, 0:1], ex[:, :, NG:NG + 1], ALU.mult))
                v.tensor_tensor(oh0[:, :, :], oh0[:, :, :], tw[:, :, 0:1].to_broadcast([P, NT, NE]), ALU.mult)
                link(v.tensor_tensor(oh1[:, :, :], oh1[:, :, :], tw[:, :, 1:2].to_broadcast([P, NT, NE]), ALU.mult))
                v.tensor_tensor(wt_tab[:, :, 0:NE], oh0[:, :, :], oh1[:, :, :], ALU.add)
                def choose(i, g):
                    blk = i * QB
                    iota_b = slots1[:, :].unsqueeze(1).unsqueeze(1).to_broadcast([P, NT, QB, BLK])
                    v.tensor_tensor(sel, pos_tab[:, :, bass.ds(blk, QB)].unsqueeze(3).to_broadcast([P, NT, QB, BLK]),
                                    iota_b, ALU.is_equal).then_inc(sel_ready, 1)
                    dve.wait_ge(sel_ready, g + l + 1)
                    v.tensor_tensor(selw, sel, wt_tab[:, :, bass.ds(blk, QB)].unsqueeze(3).to_broadcast([P, NT, QB, BLK]),
                                    ALU.mult).then_inc(selw_ready, 1)

                dve.wait_ge(rank_ps, l + 1)
                rk = psD[:, 0, 0:2 * NE].rearrange("p (t e) -> p t e", t=NT)
                link(v.scalar_tensor_tensor(pos_tab[:, :, 0:NE], rk, 1.0, member[:, :, :], ALU.add, ALU.mult))
                choose(0, start)
                nb = S // BLK - 1
                link(v.tensor_tensor(beyond[:, :, :], psD[:, 0, 2 * NE:3 * NE].unsqueeze(2).to_broadcast([P, NE, nb]),
                                     thresholds[:, :].unsqueeze(1).to_broadcast([P, NE, nb]), ALU.is_gt))
                link(v.tensor_reduce(cumA[:, 16:], beyond[:, :, :], AX.X, ALU.add))
                link(v.tensor_reduce(total[:, :], cumA[:, 16:], AX.X, ALU.add))
                link(v.tensor_scalar(npair[:, :], bidx[:, 0:OVER_BLOCKS:QB], total[:, 0:1], None, ALU.is_lt))
                link(v.tensor_reduce(total[:, :], npair[:, :], AX.X, ALU.add))
                link(v.scalar_tensor_tensor(pairs_f[:, :], total[:, :], float(MAIN_PAIRS), pairs_f[:, :], ALU.add, ALU.add))
                v.tensor_copy(pairs_i[:, bass.ds(l + 1, 1)], pairs_f[:, :]).then_inc(pairs_known, 1)

                def gathered(g):
                    for b in range(2):
                        dve.wait_ge(gather_ps, (g + l) * 2 + b + 1)
                        v.tensor_tensor(xT[:, 4 * b:4 * b + 4, :], psA[:, b, :].rearrange("p (c n) -> p c n", c=4),
                                              g_ffn[:, 4 * b:4 * b + 4].unsqueeze(2).to_broadcast([P, 4, P]), ALU.mult).then_inc(xT_done, 1)

                def add_rows(g, last=False):
                    for t in range(NT):
                        dve.wait_ge(scatter_ps[t], g + 1)
                        v.tensor_tensor(x[:, t, :].rearrange("p (b n) -> p b n", b=2), x[:, t, :].rearrange("p (b n) -> p b n", b=2),
                                        (psB if last and t else psA)[:, :, :], ALU.add).then_inc(x_added, 1)

                def choose_next(i, g):
                    dve.wait_ge(selT_ps, g + 1)
                    choose(i + 1, g + 1)

                def pair_rest(g):
                    dve.wait_ge(pair_freed, g * STAGES + STAGES + 4)
                    dve.wait_ge(silu_act, g + 1)
                    v.tensor_tensor(hid, silu, psB[:, 1, :], ALU.mult).then_inc(hid_done, 1)
                    gathered(g + 1)
                    dve.wait_ge(pair_freed, g * STAGES + 2 * STAGES)
                    v.tensor_copy(y[:, 1, :], psC[:, 1, :]).then_inc(y_dve, 1)

                def overflow_tables():
                    src, dst = cumA, cumB
                    for s in (1, 2, 4, 8, 16):
                        link(v.tensor_tensor(dst[:, 16:], src[:, 16:], src[:, 16 - s:16 + NE - s], ALU.add))
                        src, dst = dst, src
                    cum = src[:, 16:].unsqueeze(1).to_broadcast([P, TAB_BLOCKS, NE])
                    link(v.tensor_tensor(over1, cum, bidx[:, :].unsqueeze(2).to_broadcast([P, TAB_BLOCKS, NE]), ALU.is_le))
                    v.tensor_reduce(over_e[:, :], over1, AX.X, ALU.add)
                    link(v.tensor_tensor(over2, over1, cum, ALU.mult))
                    link(v.tensor_reduce(over_prev[:, :], over2, AX.X, ALU.max))
                    link(v.tensor_tensor(over_prev[:, :], bidx[:, :], over_prev[:, :], ALU.subtract))
                    v.tensor_scalar(over_prev[:, :], over_prev[:, :], 1.0, float(BLK), ALU.add, ALU.mult)
                    v.tensor_scalar(over_i[:, :], over_e[:, :], float(NE - 1), None, ALU.min).then_inc(over_known, 1)
                    link(v.tensor_tensor(over1, iota[:, :].unsqueeze(1).to_broadcast([P, TAB_BLOCKS, NE]),
                                         over_e[:, :].unsqueeze(2).to_broadcast([P, TAB_BLOCKS, NE]), ALU.is_equal))
                    for t in range(NT):
                        link(v.tensor_tensor(over2, over1, pos_tab[:, t:t + 1, 0:NE].to_broadcast([P, TAB_BLOCKS, NE]), ALU.mult))
                        link(v.tensor_reduce(over_r[:, :], over2, AX.X, ALU.add))
                        v.tensor_tensor(pos_tab[:, t, NE:], over_r[:, :], over_prev[:, :], ALU.subtract)
                        link(v.tensor_tensor(over2, over1, wt_tab[:, t:t + 1, 0:NE].to_broadcast([P, TAB_BLOCKS, NE]), ALU.mult))
                        link(v.tensor_reduce(wt_tab[:, t, NE:], over2, AX.X, ALU.add))

                dve.wait_ge(pairs_known, l + 2)
                alone(dve)
                end = dve.value_load(pairs_i[0:1, bass.ds(l + 1, 1)], min_val=MAIN_PAIRS, max_val=DEPTH * MAX_PAIRS)
                gathered(start)
                choose_next(0, start)
                overflow_tables()
                pair_rest(start)
                with dve.Fori(0, nc.s_assert_within(end - start - 1, MAIN_PAIRS - 1, MAX_PAIRS - 1)) as i:
                    add_rows(start + i)
                    choose_next(i + 1, start + i + 1)
                    pair_rest(start + i + 1)
                add_rows(end - 1, last=True)
                dve.wait_ge(x_added, end * 2 + 1)
                assert linked[0] == DVE_MIX, f"DVE_MIX = {linked[0]}"

            link_n = [0]

            def last(ins):
                link_n[0] += 1
                ins.then_inc(final_link, 1)
                dve.wait_ge(final_link, link_n[0])

            last(v.tensor_tensor_reduce(xn[:, D:2 * D], x[:, 1, :], x[:, 1, :], 1.0, 0.0, ALU.mult, ALU.add, ss[:, 1:2]))
            dve.wait_ge(ss_act, 2 * DEPTH + 1)
            variance(ss[:, :], 1.0 / D, last)
            last(newton_step(3 * DEPTH + 1, last))
            dve.wait_ge(gfin_landed, 16)
            for t in range(NT):
                v.scalar_tensor_tensor(xn[:, t * D:(t + 1) * D], x[:, t, :], rstd[:, t:t + 1], gfin[:, :],
                                       ALU.mult, ALU.mult).then_inc(final_done, 1)

        def tensor_program(pe):
            te = nc.tensor
            pe.wait_ge(consts, 3)
            pe.wait_ge(rows_landed, 32)
            n_rows = rows.shape[0]
            te.transpose(psD[:, 1, 0:n_rows], rows[:, :], ident[0:n_rows, 0:n_rows]).then_inc(cols_ps, 1)
            pe.wait_ge(setup_done, 1)
            with pe.Fori(0, DEPTH) as l:
                pe.wait_ge(pairs_known, l + 1)
                alone(pe)
                done = pe.value_load(pairs_i[0:1, bass.ds(l, 1)], min_val=0, max_val=DEPTH * MAX_PAIRS)

                def split(p):
                    pe.wait_ge(low_dve, l * MIX_SLOTS + p - PAD + 1)
                    return [w.rearrange("p (c n) -> p c n", c=4) for w in high_and_low(p)]

                TERMS = ((0, 0), (0, 1), (1, 0))

                def product(o, xs, ws, weights_stationary, start, stop):
                    for i, (a, b) in enumerate(TERMS):
                        first, second = (ws[b], xs[a]) if weights_stationary else (xs[a], ws[b])
                        ins = te.matmul(o, first, second, start=start and i == 0, stop=stop and i == len(TERMS) - 1)
                    return ins

                def free_result(n):
                    if n < 2:
                        return
                    if n - 2 in on_act:
                        pe.wait_ge(act_out, l * len(on_act) + 1 + on_act.index(n - 2))
                    else:
                        pe.wait_ge(dve_out, l * len(on_dve) + 1 + on_dve.index(n - 2))

                def norm_transposes(which):
                    if which == 0:
                        pe.wait_ge(xn_act, l * 2 + 1)
                        pe.wait_ge(xn_dve, l + 1)
                    else:
                        pe.wait_ge(dve_out, (l + 1) * len(on_dve))
                    for b in range(4):
                        ps = (psA, psB)[b // 2]
                        for c in range(2):
                            m = 2 * b + c
                            for t in range(NT):
                                src = xn[:, t * D + m * P:t * D + (m + 1) * P] if which == 0 else x[:, t, m::KC]
                                ins = te.transpose(ps[:, b % 2, c * S + t * P:c * S + t * P + P], src, ident[:, :])
                        ins.then_inc(hT_ps, 1)

                def group(g):
                    token_major = g in (G_QI, G_Q, G_K, G_V, G_VA)
                    n = N_IDX if g == G_QI else WB
                    ps = (psA, psB)[g % 2]
                    w = [split(p) for p in unit_slots(g)]
                    if g == G_QI:
                        pe.wait_ge(hT_dve, l * 6 + 2)
                    free_result(g)
                    for m in range(NT if token_major else 4):
                        for c in range(KC):
                            ends = c == 0, c == KC - 1
                            if g == G_QI and m == 0 and c in (4, 6):
                                pe.wait_ge(hT_dve, l * 6 + c // 2 + 1)
                            if token_major:
                                ins = product(ps[:, m, 0:n], [h[:, c, m * P:(m + 1) * P] for h in (hT_high, hT_low)],
                                              [wp[:, c % 4, :] for wp in w[c // 4]], False, *ends)
                            else:
                                ins = product(ps[:, m // 2, (m % 2) * S:(m % 2 + 1) * S], [h[:, c, :] for h in (hT_high, hT_low)],
                                              [wp[:, c % 4, m * P:(m + 1) * P] for wp in w[c // 4]], True, *ends)
                    ins.then_inc(mixed, 1)

                def index_transposes():
                    pe.wait_ge(idx_roped, l + 1)
                    for a in range(3):
                        for t in range(NT):
                            o = psC[:, 0, a * S + t * P:a * S + t * P + P] if a < 2 else psC[:, 1, t * P:t * P + P]
                            ins = te.transpose(o, idx[:, t, a * P:(a + 1) * P], ident[:, :])
                    ins.then_inc(idxT_ps, 1)

                def index_scores():
                    pe.wait_ge(idxT_act, l + 1)
                    for b, ps, nk in ((0, psD, P), (1, psC, S)):
                        for h in range(IH):
                            r = h % 2
                            a = h // 2
                            ins = te.matmul(ps[:, r, a * nk:(a + 1) * nk], qiT[IDIM * r:IDIM * (r + 1), a, b * P:(b + 1) * P],
                                            kiT[IDIM * r:IDIM * (r + 1), 0:nk], start=True, stop=True)
                        ins.then_inc(score_ps, 1)

                def head_transposes(src, ps, ready, freed, done_sem):
                    pe.wait_ge(ready, l + 1)
                    freed()
                    for h in range(HEADS):
                        for t in range(NT):
                            o = (h % 2) * S + t * P
                            ins = te.transpose(ps[:, h // 2, o:o + P], src[:, t, h * HD:(h + 1) * HD], ident[:, :])
                    ins.then_inc(done_sem, 1)

                def logits():
                    pe.wait_ge(qT_act, l + 1)
                    pe.wait_ge(kT_act, l + 1)
                    for h in range(HEADS):
                        ins = te.matmul(psD[:, 0, h * P:(h + 1) * P], qT[:, h, 0:P], kT[:, h, 0:P], start=True, stop=True)
                    ins.then_inc(logit_ps, 1)
                    for h in range(HEADS):
                        ins = te.matmul(psC[:, h // 2, (h % 2) * S:(h % 2 + 1) * S], qT[:, h, P:S], kT[:, h, :], start=True, stop=True)
                    ins.then_inc(logit_ps, 1)

                def prob_transposes():
                    pe.wait_ge(probs, l * 2 + 1)
                    for h in range(HEADS):
                        ins = te.transpose(psD[:, 1, h * P:(h + 1) * P], p0[:, h, :], ident[:, :])
                    ins.then_inc(pT_ps, 1)
                    pe.wait_ge(probs, l * 2 + 2)
                    for k in range(2):
                        for h in range(HEADS):
                            ins = te.transpose(psC[:, k, h * P:(h + 1) * P], rel[:, h, k * P:(k + 1) * P], ident[:, :])
                    ins.then_inc(pT_ps, 1)

                def attend():
                    pe.wait_ge(pT_act, l + 1)
                    for h in range(HEADS):
                        o = (h % 2) * S
                        te.matmul(psD[:, h // 2, o:o + P], v_tok[:, 0, h * HD:(h + 1) * HD], pT[:, 0, h, :], start=True, stop=True)
                        for k in range(2):
                            ins = te.matmul(psD[:, h // 2, o + P:o + S], v_tok[:, k, h * HD:(h + 1) * HD], pT[:, 1 + k, h, :],
                                            start=k == 0, stop=k == 1)
                    ins.then_inc(ybT_ps, 1)

                def spatial_transposes():
                    pe.wait_ge(ws_landed, l * 32 + 32)
                    for h in range(HEADS):
                        ins = te.transpose(psC[:, 0, h * P:(h + 1) * P], ws_raw[:, h, :], ident[:, :])
                    ins.then_inc(wsT_ps, 1)

                def spatial():
                    pe.wait_ge(tri_done, l + 1)
                    pe.wait_ge(v_normed, l + 1)
                    for h in range(HEADS):
                        for t in range(NT):
                            o = psC[:, h // 2, (h % 2) * S + t * P:(h % 2) * S + (t + 1) * P]
                            te.matmul(o, vg[:, t, h * HD:(h + 1) * HD], wsT[:, h, :], start=True, stop=False)
                            ins = te.matmul(o, ones[0:1, :], bs_row[0:1, h * P:(h + 1) * P], start=False, stop=True)
                    ins.then_inc(vm_ps, 1)

                norm_transposes(0)
                group(G_QI)
                group(G_Q)
                index_transposes()
                group(G_K)
                index_scores()
                group(G_V)
                head_transposes(q_tok, psD, q_roped, lambda: pe.wait_ge(rel_act, l * 2 + 1), qT_ps)
                group(G_VA)
                head_transposes(k_tok, psC, k_roped, lambda: pe.wait_ge(rel_act, l * 2 + 2), kT_ps)
                group(G_U)
                logits()
                group(G_CX)
                group(G_CC)
                prob_transposes()
                group(G_CB)
                attend()
                spatial_transposes()
                group(G_GATE0)
                group(G_GATE0 + 1)
                spatial()
                for n in range(2, 6):
                    group(G_GATE0 + n)

                for k in range(N_PROJ):
                    n = N_IN + k
                    p = PAD + 2 * N_IN + k
                    branch = k % 3
                    if k == 0:
                        pe.wait_ge(branch_low_dve, l * 3 + 3)
                    w = split(p)
                    free_result(n)
                    for m in range(4):
                        for c in range(4):
                            ins = product((psA, psB)[n % 2][:, m // 2, (m % 2) * S:(m % 2 + 1) * S],
                                          [part[:, c, :] for part in (branch_high[branch], branch_low[branch])],
                                          [wp[:, c, m * P:(m + 1) * P] for wp in w], True, c == 0, c == 3)
                    ins.then_inc(mixed, 1)
                for part in range(2):
                    for half in range(2):
                        n = N_IN + N_PROJ + half
                        w = split(P_OUT[part, half])
                        if part == 0:
                            free_result(n)
                        if half == 0:
                            pe.wait_ge(merged_low_dve, l * 2 + part + 1)
                        for t in range(NT):
                            for c in range(4):
                                m = 4 * part + c
                                ins = product((psA, psB)[n % 2][:, t, :], [h[:, m, t * P:(t + 1) * P] for h in (merged_high, merged_low)],
                                              [wp[:, c, :] for wp in w], False, m == 0, m == KC - 1)
                        if part == 1:
                            ins.then_inc(mixed, 1)

                norm_transposes(1)
                for c in range(KC):
                    if c % 4 == 0:
                        pe.wait_ge(hT_act, l * 6 + 4 + c // 4 + 1)
                    if c % 4 == 2:
                        pe.wait_ge(hT_dve, l * 6 + 4 + c // 4 + 1)
                    for t in range(NT):
                        ins = te.matmul(psC[:, t, 0:N_ROUTE], hT[:, c, t * P:(t + 1) * P], r_w[:, c, :],
                                        start=c == 0, stop=c == KC - 1)
                ins.then_inc(route_ps, 1)
                pe.wait_ge(members, l + 1)
                for o, w, t, start, stop in ((0, before_r, 0, True, True), (1, ones_r, 0, True, False), (1, before_r, 1, False, True),
                                             (2, ones_r, 0, True, False), (2, ones_r, 1, False, True)):
                    ins = te.matmul(psD[:, 0, o * NE:(o + 1) * NE], w[:, :], member[:, t, :], start=start, stop=stop)
                ins.then_inc(rank_ps, 1)

                def expert_arrived(g, p):
                    s = p % SLOTS
                    pe.wait_ge(landed[s], l * (16 * MIX_USES[s]) + g * 16 + 16 * (MIX_USES[s] + 1))

                def gather(b):
                    for c in range(4 * b, 4 * b + 4):
                        for t in range(NT):
                            o = t * D + c * P
                            ins = te.matmul(psA[:, b, (c % 4) * P:(c % 4 + 1) * P], xn[:, o:o + P],
                                            sel[:, t].rearrange("p j n -> p (j n)"), start=t == 0, stop=t == NT - 1)
                    ins.then_inc(gather_ps, 1)

                def gate_up(g, k):
                    half, o = k // 2, k % 2
                    for j in range(QB):
                        expert_arrived(g, k * QB + j)
                    for c in range(4):
                        for j in range(QB):
                            w = slot(k * QB + j, SLOT).rearrange("p (c n) -> p c n", c=4)
                            ins = te.matmul(psB[j * BLK:(j + 1) * BLK, o, :], xT[:, 4 * half + c, j * BLK:(j + 1) * BLK], w[:, c, :],
                                            start=half == 0 and c == 0, stop=half == 1 and c == 3)
                    ins.then_inc(pair_freed, 1)

                def down(g, k):
                    for j in range(QB):
                        expert_arrived(g, (4 + k) * QB + j)
                    for c in range(2):
                        for n in range(2):
                            for j in range(QB):
                                w = slot((4 + k) * QB + j, SLOT).rearrange("p (c n) -> p c n", c=2)
                                ins = te.matmul(psC[j * BLK:(j + 1) * BLK, n, :], hidT[:, 2 * k + c, j * BLK:(j + 1) * BLK],
                                                w[:, c, n * 512:(n + 1) * 512], start=k == 0 and c == 0, stop=k == 1 and c == 1)
                    ins.then_inc(pair_freed, 1)

                def scatter(g, t, last=False):
                    ps = psB if last and t else psA
                    if t == 0:
                        pe.wait_ge(selT_act, g + 1)
                        pe.wait_ge(y_act, g + 1)
                        pe.wait_ge(y_dve, g + 1)
                    elif not last:
                        pe.wait_ge(x_added, g * 2 + 2)
                    for n in range(2):
                        ins = te.matmul(ps[:, n, :], selwT[:, t, :], y[:, n, :], start=True, stop=True)
                    ins.then_inc(scatter_ps[t], 1)

                def pair(g, first):
                    pe.wait_ge(xT_done, (g + l) * 2 + 1)
                    gate_up(g, 0)
                    pe.wait_ge(xT_done, (g + l) * 2 + 2)
                    if not first:
                        scatter(g - 1, 0)
                    gate_up(g, 1)
                    if not first:
                        scatter(g - 1, 1)
                    pe.wait_ge(selw_ready, g + l + 1)
                    for t in range(NT):
                        ins = te.transpose(psD[:, 1, t * P:(t + 1) * P], selw[:, t].rearrange("p j n -> p (j n)"), ident[:, :])
                    ins.then_inc(selT_ps, 1)
                    gate_up(g, 2)
                    gate_up(g, 3)
                    pe.wait_ge(sel_ready, g + l + 2)
                    pe.wait_ge(x_added, g * 2 + 1)
                    gather(0)
                    pe.wait_ge(hid_done, g + 1)
                    for c in range(FC):
                        ins = te.transpose(psD[:, 0, c * P:(c + 1) * P], hid[:, c::FC], ident[:, :])
                    ins.then_inc(hidT_ps, 1)
                    gather(1)
                    pe.wait_ge(hidT_act, g + 1)
                    for k in range(2):
                        down(g, k)

                pe.wait_ge(xn_act, l * 2 + 2)
                pe.wait_ge(sel_ready, done + l + 1)
                gather(0)
                gather(1)
                pe.wait_ge(pairs_known, l + 2)
                alone(pe)
                end = pe.value_load(pairs_i[0:1, bass.ds(l + 1, 1)], min_val=MAIN_PAIRS, max_val=DEPTH * MAX_PAIRS)
                pair(done, True)
                with pe.Fori(done + 1, end) as g:
                    pair(g, False)
                for t in range(NT):
                    scatter(end - 1, t, last=True)


        @block.sync
        def _(sp):
            sync_program(sp)

        @block.gpsimd
        def _(pool):
            pool_program(pool)

        @block.scalar
        def _(act):
            scalar_program(act)

        @block.vector
        def _(dve):
            vector_program(dve)

        @block.tensor
        def _(pe):
            tensor_program(pe)


_INS = ['x', 'positions', 'norm_mix_g', 'norm_ffn_g', 'norm_final_g', 'w_in', 'gmlp_ws', 'gmlp_b', 'conv_w',
        'w_proj_a', 'w_proj_b', 'w_proj_c', 'w_out', 'router_group_w', 'router_group_b',
        'router_expert_w', 'router_expert_b', 'expert_w_gate', 'expert_w_up', 'expert_w_down']


def kernel(**inputs):
    import concourse.bacc as _bacc
    from concourse.bass_utils import run_bass_kernel_spmd as _run

    nc = _bacc.Bacc("TRN2", target_bir_lowering=False, num_devices=1)
    arrays, args = {}, []
    for name in _INS:
        a = np.ascontiguousarray(inputs[name])
        arrays[f"in_{name}_dram"] = a
        args.append(nc.dram_tensor(f"in_{name}_dram", a.shape, mybir.dt.from_np(a.dtype), kind="ExternalInput").ap())
    shape = tuple(inputs['x'].shape)
    args.append(nc.dram_tensor("out_0_dram", shape, F32, kind="ExternalOutput").ap())
    build_trunk(nc, *args)
    r = _run(nc, [arrays], core_ids=[0])
    return r.results[0]["out_0_dram"]
```
